# Optimizing a Trainium2 kernel written in Bass

```python
import math
import jax, jax.numpy as jnp
from jax import lax
import numpy as np

D_MODEL = 1024
BATCH = 1
SEQ = 2048
DEPTH = 1
DEC_BATCH = 1
DEC_SEQ = 32
PAST_LEN = 128

CHUNK = 64
EPS = 1e-6
LRU_W = D_MODEL // 2
LRU_HEADS = 8
LRU_HD = LRU_W // LRU_HEADS
CONV_W = 4
LRU_C = 8.0
SSM_W = D_MODEL - LRU_W
SSM_H = 16
SSM_G = SSM_W // SSM_H
SSM_P = 64
MIX_W = LRU_W + SSM_W
IN_W = 2 * LRU_W + SSM_W
D_FF = -(-8 * D_MODEL // (3 * 256)) * 256

kernel_name = "hymba_rglru_s5_streaming_step"

def _rmsnorm(x, g):
    xf = x.astype(jnp.float32)
    var = jnp.mean(xf * xf, axis=-1, keepdims=True)
    return (xf * lax.rsqrt(var + EPS) * g.astype(jnp.float32)).astype(x.dtype)

def _causal_conv(x, buf, w, b):
    T = x.shape[1]
    xp = jnp.concatenate([buf.astype(x.dtype), x], axis=1)
    y = b.astype(x.dtype)
    for k in range(CONV_W):
        y = y + xp[:, k:k + T] * w[k].astype(x.dtype)
    return y, xp[:, T:]

def _lin_combine(e1, e2):
    a1, b1 = e1
    a2, b2 = e2
    return (a1 * a2, a2 * b1 + b2)

def _rglru(xc, h0, wa, ba, wx, bx, lam):
    B_, T, W = xc.shape
    xf = xc.astype(jnp.float32)
    xh = xf.reshape(B_, T, LRU_HEADS, LRU_HD)
    r = jax.nn.sigmoid(jnp.einsum('bthi,hij->bthj', xh, wa.astype(jnp.float32)).reshape(B_, T, W) + ba.astype(jnp.float32))
    ig = jax.nn.sigmoid(jnp.einsum('bthi,hij->bthj', xh, wx.astype(jnp.float32)).reshape(B_, T, W) + bx.astype(jnp.float32))
    log_a = -LRU_C * r * jax.nn.softplus(-lam.astype(jnp.float32))
    a = jnp.exp(log_a)
    b = jnp.sqrt(-jnp.expm1(2.0 * log_a)) * (ig * xf)
    b = b.at[:, 0].add(a[:, 0] * h0.astype(jnp.float32))
    _, h = lax.associative_scan(_lin_combine, (a, b), axis=1)
    return h, h[:, -1]

def _cplx_combine(e1, e2):
    a1r, a1i, b1r, b1i = e1
    a2r, a2i, b2r, b2i = e2
    return (a2r * a1r - a2i * a1i, a2r * a1i + a2i * a1r,
            a2r * b1r - a2i * b1i + b2r, a2r * b1i + a2i * b1r + b2i)

def _s5(u, h_re, h_im, lam_re, lam_im, b_re, b_im, c_re, c_im, d, log_dt):
    B_, T, _ = u.shape
    f32 = jnp.float32
    uf = u.astype(f32)
    lr, li = lam_re.astype(f32), lam_im.astype(f32)
    dt = jnp.exp(log_dt.astype(f32))[:, None]
    mag = jnp.exp(lr * dt)
    lbr, lbi = mag * jnp.cos(li * dt), mag * jnp.sin(li * dt)
    nr, ni = lbr - 1.0, lbi
    den = lr * lr + li * li
    gr, gi = (nr * lr + ni * li) / den, (ni * lr - nr * li) / den
    br, bi = b_re.astype(f32), b_im.astype(f32)
    bbr = gr[..., None] * br - gi[..., None] * bi
    bbi = gr[..., None] * bi + gi[..., None] * br
    cr, ci = c_re.astype(f32), c_im.astype(f32)
    blk = CHUNK if T >= CHUNK else T
    n = T // blk
    uc = uf.reshape(B_, n, blk, SSM_G, SSM_H).transpose(1, 0, 2, 3, 4)

    def step(carry, u_blk):
        hr, hi = carry
        bur = jnp.einsum('blgh,gph->blgp', u_blk, bbr)
        bui = jnp.einsum('blgh,gph->blgp', u_blk, bbi)
        bur = bur.at[:, 0].add(lbr * hr - lbi * hi)
        bui = bui.at[:, 0].add(lbr * hi + lbi * hr)
        ar = jnp.broadcast_to(lbr, bur.shape)
        ai = jnp.broadcast_to(lbi, bui.shape)
        _, _, xr, xi = lax.associative_scan(_cplx_combine, (ar, ai, bur, bui), axis=1)
        y = jnp.einsum('ghp,blgp->blgh', cr, xr) - jnp.einsum('ghp,blgp->blgh', ci, xi)
        return (xr[:, -1], xi[:, -1]), y

    (hr, hi), ys = lax.scan(step, (h_re.astype(f32), h_im.astype(f32)), uc)
    y = ys.transpose(1, 0, 2, 3, 4).reshape(B_, T, SSM_W) + d.astype(f32) * uf
    return y, hr, hi

def _layer(x, conv_buf, lru_h, ssm_re, ssm_im, p):
    dt = x.dtype
    h = _rmsnorm(x, p['norm_mix'])
    z = jnp.einsum('btd,de->bte', h, p['w_in'])
    xl = z[..., :LRU_W]
    gl = z[..., LRU_W:2 * LRU_W]
    us = z[..., 2 * LRU_W:]
    xc, new_conv = _causal_conv(xl, conv_buf, p['conv_w'], p['conv_b'])
    hl, new_lru = _rglru(xc, lru_h, p['lru_wa'], p['lru_ba'], p['lru_wx'], p['lru_bx'], p['lru_lambda'])
    y_lru = (hl * jax.nn.gelu(gl.astype(jnp.float32))).astype(dt)
    ys, new_re, new_im = _s5(us, ssm_re, ssm_im, p['ssm_lambda_re'], p['ssm_lambda_im'], p['ssm_b_re'], p['ssm_b_im'],
                             p['ssm_c_re'], p['ssm_c_im'], p['ssm_d'], p['ssm_log_dt'])
    g = jax.nn.gelu(ys)
    y_ssm = (g * jax.nn.sigmoid(jnp.einsum('bte,ef->btf', g, p['ssm_w_glu'].astype(jnp.float32)) + p['ssm_b_glu'].astype(jnp.float32))).astype(dt)
    mix = jnp.concatenate([_rmsnorm(y_lru, p['norm_lru_out']), _rmsnorm(y_ssm, p['norm_ssm_out'])], axis=-1)
    x = x + jnp.einsum('bte,ed->btd', mix, p['w_out'])
    h2 = _rmsnorm(x, p['norm_ffn'])
    ff = jax.nn.silu(jnp.einsum('btd,df->btf', h2, p['w_gate'])) * jnp.einsum('btd,df->btf', h2, p['w_up'])
    x = x + jnp.einsum('btf,fd->btd', ff, p['w_down'])
    return x, new_conv, new_lru, new_re, new_im

def setup_inputs(seed: int = 0) -> dict:
    key = jax.random.key(seed)
    ks = jax.random.split(key, 40)
    f32 = jnp.float32

    def nrm(k, shape, scale):
        return jax.random.normal(k, shape, f32) * scale

    def gain(k, shape):
        return 1.0 + 0.02 * jax.random.normal(k, shape, f32)

    a0 = jax.random.uniform(ks[14], (DEPTH, LRU_W), f32, 0.9, 0.999)
    lam_im_base = jnp.pi * jnp.arange(SSM_P, dtype=f32)
    return {
        "x_prompt": nrm(ks[0], (BATCH, SEQ, D_MODEL), 1.0),
        "x_sample": nrm(ks[1], (DEC_BATCH, DEC_SEQ, D_MODEL), 1.0),
        "state_conv": nrm(ks[2], (DEPTH, DEC_BATCH, CONV_W - 1, LRU_W), 1.0),
        "state_lru": nrm(ks[3], (DEPTH, DEC_BATCH, LRU_W), 0.5),
        "state_ssm_re": nrm(ks[4], (DEPTH, DEC_BATCH, SSM_G, SSM_P), 0.5),
        "state_ssm_im": nrm(ks[5], (DEPTH, DEC_BATCH, SSM_G, SSM_P), 0.5),
        "norm_mix": gain(ks[6], (DEPTH, D_MODEL)),
        "w_in": nrm(ks[7], (DEPTH, D_MODEL, IN_W), D_MODEL ** -0.5),
        "conv_w": nrm(ks[8], (DEPTH, CONV_W, LRU_W), CONV_W ** -0.5),
        "conv_b": nrm(ks[9], (DEPTH, LRU_W), 0.01),
        "lru_wa": nrm(ks[10], (DEPTH, LRU_HEADS, LRU_HD, LRU_HD), LRU_HD ** -0.5),
        "lru_ba": nrm(ks[11], (DEPTH, LRU_W), 0.01),
        "lru_wx": nrm(ks[12], (DEPTH, LRU_HEADS, LRU_HD, LRU_HD), LRU_HD ** -0.5),
        "lru_bx": nrm(ks[13], (DEPTH, LRU_W), 0.01),
        "lru_lambda": jnp.log(a0) - jnp.log1p(-a0),
        "ssm_lambda_re": -0.5 + nrm(ks[15], (DEPTH, SSM_G, SSM_P), 0.01),
        "ssm_lambda_im": lam_im_base + nrm(ks[16], (DEPTH, SSM_G, SSM_P), 0.01),
        "ssm_b_re": nrm(ks[17], (DEPTH, SSM_G, SSM_P, SSM_H), (2 * SSM_H) ** -0.5),
        "ssm_b_im": nrm(ks[18], (DEPTH, SSM_G, SSM_P, SSM_H), (2 * SSM_H) ** -0.5),
        "ssm_c_re": nrm(ks[19], (DEPTH, SSM_G, SSM_H, SSM_P), SSM_P ** -0.5),
        "ssm_c_im": nrm(ks[20], (DEPTH, SSM_G, SSM_H, SSM_P), SSM_P ** -0.5),
        "ssm_d": nrm(ks[21], (DEPTH, SSM_W), 0.5),
        "ssm_log_dt": jax.random.uniform(ks[22], (DEPTH, SSM_G), f32, math.log(0.001), math.log(0.1)),
        "ssm_w_glu": nrm(ks[23], (DEPTH, SSM_W, SSM_W), SSM_W ** -0.5),
        "ssm_b_glu": nrm(ks[24], (DEPTH, SSM_W), 0.01),
        "norm_lru_out": gain(ks[25], (DEPTH, LRU_W)),
        "norm_ssm_out": gain(ks[26], (DEPTH, SSM_W)),
        "w_out": nrm(ks[27], (DEPTH, MIX_W, D_MODEL), MIX_W ** -0.5),
        "norm_ffn": gain(ks[28], (DEPTH, D_MODEL)),
        "w_gate": nrm(ks[29], (DEPTH, D_MODEL, D_FF), D_MODEL ** -0.5),
        "w_up": nrm(ks[30], (DEPTH, D_MODEL, D_FF), D_MODEL ** -0.5),
        "w_down": nrm(ks[31], (DEPTH, D_FF, D_MODEL), D_FF ** -0.5),
        "norm_final": gain(ks[32], (D_MODEL,)),
    }

def reference(x_prompt, x_sample, state_conv, state_lru, state_ssm_re, state_ssm_im,
              norm_mix, w_in, conv_w, conv_b, lru_wa, lru_ba, lru_wx, lru_bx, lru_lambda,
              ssm_lambda_re, ssm_lambda_im, ssm_b_re, ssm_b_im, ssm_c_re, ssm_c_im, ssm_d, ssm_log_dt,
              ssm_w_glu, ssm_b_glu, norm_lru_out, norm_ssm_out, w_out, norm_ffn, w_gate, w_up, w_down,
              norm_final):
    bp = x_prompt.shape[0]
    conv0 = jnp.zeros((bp, CONV_W - 1, LRU_W), x_prompt.dtype)
    lru0 = jnp.zeros((bp, LRU_W), jnp.float32)
    re0 = jnp.zeros((bp, SSM_G, SSM_P), jnp.float32)
    im0 = jnp.zeros((bp, SSM_G, SSM_P), jnp.float32)
    yp, ys = x_prompt, x_sample
    pc, pl, pr, pi_, sc, sl, sr, si = [], [], [], [], [], [], [], []
    for l in range(DEPTH):
        p = {
            'norm_mix': norm_mix[l], 'w_in': w_in[l], 'conv_w': conv_w[l], 'conv_b': conv_b[l],
            'lru_wa': lru_wa[l], 'lru_ba': lru_ba[l], 'lru_wx': lru_wx[l], 'lru_bx': lru_bx[l],
            'lru_lambda': lru_lambda[l], 'ssm_lambda_re': ssm_lambda_re[l], 'ssm_lambda_im': ssm_lambda_im[l],
            'ssm_b_re': ssm_b_re[l], 'ssm_b_im': ssm_b_im[l], 'ssm_c_re': ssm_c_re[l], 'ssm_c_im': ssm_c_im[l],
            'ssm_d': ssm_d[l], 'ssm_log_dt': ssm_log_dt[l], 'ssm_w_glu': ssm_w_glu[l], 'ssm_b_glu': ssm_b_glu[l],
            'norm_lru_out': norm_lru_out[l], 'norm_ssm_out': norm_ssm_out[l], 'w_out': w_out[l],
            'norm_ffn': norm_ffn[l], 'w_gate': w_gate[l], 'w_up': w_up[l], 'w_down': w_down[l],
        }
        yp, c1, h1, r1, i1 = _layer(yp, conv0, lru0, re0, im0, p)
        ys, c2, h2, r2, i2 = _layer(ys, state_conv[l], state_lru[l], state_ssm_re[l], state_ssm_im[l], p)
        pc.append(c1); pl.append(h1); pr.append(r1); pi_.append(i1)
        sc.append(c2.astype(state_conv.dtype)); sl.append(h2.astype(state_lru.dtype))
        sr.append(r2.astype(state_ssm_re.dtype)); si.append(i2.astype(state_ssm_im.dtype))
    y_prompt = _rmsnorm(yp, norm_final)
    y_sample = _rmsnorm(ys, norm_final)
    return (y_prompt, y_sample,
            jnp.stack(pc), jnp.stack(pl), jnp.stack(pr), jnp.stack(pi_),
            jnp.stack(sc), jnp.stack(sl), jnp.stack(sr), jnp.stack(si))


_drawn_inputs = setup_inputs


def setup_inputs(seed=0):
    import zlib

    import numpy as np

    out = dict(_drawn_inputs(seed))
    spreads = {}
    factors = {'lru_ba': 8.0,
     'lru_bx': 8.0,
     'ssm_lambda_re': 55.717,
     'ssm_b_glu': 8.0,
     'norm_lru_out': 53.669,
     'norm_ssm_out': 60.748,
     'norm_ffn': 13.37,
     'norm_final': 20.24}
    for name, (base, spread) in spreads.items():
        noise = np.random.default_rng([zlib.crc32(name.encode()), seed]).standard_normal(out[name].shape)
        drawn = base * np.exp(spread * noise) if base else spread * noise
        out[name] = __import__('jax').numpy.asarray(drawn.astype(out[name].dtype))
    for name, factor in factors.items():
        out[name] = (out[name] * factor).astype(out[name].dtype)
    return out
```

```python
import math
from contextlib import ExitStack

import concourse.bass as bass
from concourse import mybir

F32 = mybir.dt.float32
F32R = mybir.dt.float32r
ALU = mybir.AluOpType
ACT = mybir.ActivationFunctionType

P = 128
D = 1024
SEQ, DEC_SEQ = 2048, 32
BLOCKS = 2
L = 8
TP, TS = SEQ // BLOCKS, DEC_SEQ // BLOCKS
PAD = L
S0 = TP + PAD
TB = S0 + TS
PIECES = [(0, 352), (352, 352), (704, TB - 704)]
NPC = len(PIECES)
NC = TB // L
CP, CS = TP // L, S0 // L
NW = NC + 1
KD = D // P
LRU_W = SSM_W = 512
KL = LRU_W // P
G, HG, NP_ = 32, 16, 64
GP = G // 2
GE = P // HG
D_FF = 2816
NF = D_FF // P
NI = NF // 2
CONV_W = 4
LRU_C = 8.0
EPS = 1e-6
ACC, AUX = 6, 2
SP5 = 5 * P + 2 * NW
NPOW = 8 + 9
LN_TERMS = 9
MAGIC = 1.5 * 2.0 ** 23
MAGIC12 = 1.5 * 2.0 ** 11
TWO_PI = 2.0 * math.pi
PI_A = 6.28125
PI_B = 0.0019350051879882812
PI_C = TWO_PI - PI_A - PI_B

IN_ORDER = [("us", 0), ("us", 1), ("us", 2), ("us", 3), ("xl", 0), ("xl", 1), ("gl", 0), ("gl", 1),
            ("xl", 2), ("xl", 3), ("gl", 2), ("gl", 3)]
PHASE1 = [("us", 0), ("us", 1), ("us", 2), ("us", 3), ("xl", 0), ("xl", 1), ("gl", 0), ("gate", 0),
          ("gl", 1), ("gate", 1), ("xl", 2), ("xl", 3), ("gl", 2), ("gate", 2), ("gl", 3), ("gate", 3)]
NSMALL = 12 + KL + KD
NORMS = ["n1", "nl", "ns", "n2", "nf"]
NCH = {"n1": KD, "nl": KL, "ns": KL, "n2": KD, "nf": KD}


def before(which, count):
    return sum(count(w) for w in NORMS[:NORMS.index(which) if which else None])


def n_sq(which):
    return 0 if which == "nl" else NCH[which]


def n_sum(which):
    return 0 if which == "nl" else NCH[which] - 1


def n_nrm(which):
    return 0 if which == "nf" else NCH[which]


def acc_order():
    order = []
    for kind, j in PHASE1:
        for p in range(NPC):
            if kind == "gate":
                order += [("r", j, p), ("ig", j, p)]
            else:
                order.append((kind, j, p))
    for t in range(GP + 2):
        if t >= 2:
            order.append(("y5", t - 2, 0))
        if t < GP:
            order += [("v1", t, 0), ("v2", t, 0)]
    order += [("glu", j, p) for j in range(KL) for p in range(NPC)]
    order += [("out", d, p) for d in range(KD) for p in range(NPC)]
    return {key: n for n, key in enumerate(order)}


ACC_AT = acc_order()
ACC_MIX = len(ACC_AT)
ACC_BLOCK = ACC_MIX + NI * 4 * NPC
AUX_AT = {key: n for n, key in enumerate(
    [("n1", 0, p) for p in range(NPC)] + [("fin", 0, 0), ("nl", 0, 0), ("nl", 0, 1), ("nl", 0, 2)]
    + [("ns", 0, p) for p in range(NPC)] + [("n2", 0, p) for p in range(NPC)])}
AUX_MIX = len(AUX_AT)
AUX_AT.update({("nf", 0, p): AUX_MIX + NI * KD * NPC + p for p in range(NPC)})
AUX_BLOCK = AUX_MIX + NI * KD * NPC + NPC
assert ACC_MIX % ACC == 0 and ACC_BLOCK % ACC == 0, (ACC_MIX, ACC_BLOCK)
assert AUX_BLOCK % AUX == 0 and (KD * NPC) % AUX == 0 and 4 * NPC % ACC == 0


def build(nc, a, outs):
    with ExitStack() as ctx:
        def sem(name):
            return ctx.enter_context(nc.semaphore(name))

        def at(name, shape, dt, offset):
            return nc.alloc_sbuf_tensor_at(name, shape, dt, offset=offset)

        top = [(nc.sbuf_base + 31) // 32 * 32]

        def take(nbytes):
            top[0] += (nbytes + 31) // 32 * 32
            return top[0] - (nbytes + 31) // 32 * 32

        def sb(name, shape, dt=F32):
            return at(name, shape, dt, take(4 * math.prod(shape[1:])))

        RB = TB * 4
        x_acc = sb("x_acc", [P, KD, TB])
        ones = sb("ones", [P, P])
        ident = sb("ident", [P, P])
        swap = sb("swap", [P, P])
        lmask = sb("lmask", [P, NW])
        w_gates = sb("w_gates", [P, 2, KL, P])
        vec = sb("vec", [P, 68])
        small = sb("small", [P, 20])
        carry5 = sb("carry5", [P, G, 2])
        rho = sb("rho", [P, G])
        fin5 = sb("fin5", [P, 2, G, 2])
        conv_st = sb("conv_st", [P, KL, 2, CONV_W - 1])
        lru_st = sb("lru_st", [P, KL, 2])
        B = take(2 * KD * RB)
        act_hl = at("act_hl", [P, 2, KD, TB], F32R, B)
        u5 = at("u5", [P, G, NC], F32, B)
        g5 = at("g5", [P, G, NC], F32, B + G * NC * 4)
        s5ring = at("s5ring", [P, 4, 2, SP5], F32, B + 2 * G * NC * 4)
        C = take(0)
        sw_raw = at("sw_raw", [P, 2, D], F32, C)
        sw_hl = at("sw_hl", [P, 2, 2, D], F32R, C + 8192)
        zs = at("zs", [P, KL, L, NC], F32, C + 24576)
        y_lru = at("y_lru", [P, KL, TB], F32, C + 24576 + 4 * RB)
        LT = C + 24576 + 8 * RB
        tmp = at("tmp", [P, 10, TB], F32, LT)
        xl = at("xl", [P, 3 + TB], F32, LT + 10 * RB)
        sig2 = at("sig2", [P, TB], F32, LT + 10 * RB)
        g_hl = at("g_hl", [P, 2, KL, TB], F32R, LT)
        s5tmp = at("s5tmp", [P, 2, 7, 2, NW], F32, LT)
        gu_hl = at("gu_hl", [P, 2, 2, 2 * D], F32R, C)
        dn_hl = at("dn_hl", [P, 2, 2, D], F32R, C + 32768)
        f_tmp = at("f_tmp", [P, 6, 352], F32, C + 49152)
        h2_tmp = at("h2_tmp", [P, 2, TB], F32, C + 49152)
        f_raw = at("f_raw", [P, 2, 3 * D], F32, LT)
        ff_hl = at("ff_hl", [P, 2, 2, TB], F32R, LT + 6 * RB)
        END = LT + 10 * RB + (3 + TB) * 4
        assert C + 49152 + 2 * RB <= LT and 6 * D * 4 <= 6 * RB and END <= nc.sbuf_usable_end, (END, nc.sbuf_usable_end)
        tb = [at(f"tb{i}", [P, G, NW], F32, B + i * G * NW * 4) for i in range(3)]
        btT = at("btT", [P, G, P], F32, B + 3 * G * NW * 4)
        pt = [at(f"pt{i}", [P, G, NPOW], F32, B + i * G * NPOW * 4) for i in range(4)]
        pz = at("pz", [P, 20, G], F32, B + 16384)
        dd = at("dd", [HG, G, HG], F32, B + 24576)
        zero = at("zero", [HG, G, 7 * HG], F32, B + 28672)
        kf = at("kf", [P, NPOW], F32, B + 43520)
        dsk = at("dsk", [HG, G], F32, B + 44544)
        SU = C + 24576
        bt = [at(f"bt{i}", [P, G, 9, HG], F32, SU + i * 18432) for i in range(2)]
        kj = at("kj", [HG, G, 8, HG], F32, SU + 2 * 18432)
        SV = SU + 2 * 18432 + 16384
        bc = at("bc", [P, 4, G, HG], F32, SV)
        bb = at("bb", [P, 4, G, HG], F32, SV + 8192)
        pw = at("pw", [P, 3, G, NPOW], F32, SV + 16384)
        jrow = at("jrow", [P, NW], F32, SV + 16384 + 3 * G * NPOW * 4)
        p5 = at("p5", [P, 3, G], F32, SV + 16384 + 3 * G * NPOW * 4 + 544)
        tau = at("tau", [P, 3, G], F32, SV + 16384 + 3 * G * NPOW * 4 + 544 + 3 * G * 4)
        assert SV + 16384 + 3 * G * NPOW * 4 + 544 + 6 * G * 4 <= nc.sbuf_usable_end

        acc = ctx.enter_context(nc.psum_tensor("acc", [P, ACC, 512], F32))
        aux = ctx.enter_context(nc.psum_tensor("aux", [P, AUX, 512], F32))
        z_dram = nc.dram_tensor("z_dram", (BLOCKS, L, HG, G, NC), F32).ap()
        g_dram = nc.dram_tensor("g_dram", (BLOCKS, L, HG, G, NC), F32).ap()
        k_dram = nc.dram_tensor("k_dram", (HG, G, 15 * HG), F32).ap()
        s5_dram = nc.dram_tensor("s5_dram", (P, G, SP5), F32).ap()

        G_MIX, G_FFN, G_FIN, G_LRU, G_SSM = 0, 8, 16, 24, 28
        B_A, B_X, B_GLU, CONV, CONVB, LAM = 32, 36, 40, 44, 60, 64
        SGN, NS2PI, HPI, CL, NCL, N2CL = 0, 1, 2, 4, 8, 12
        btmp = at("btmp", [P, 4, TB], F32, B + 4 * RB)

        def v1(c):
            return vec[:, c:c + 1]

        def sm(c):
            return small[:, c:c + 1]

        par_in = sem("par_in")
        consts = sem("consts")
        dt_done, ang_done, pow_done = sem("dt_done"), sem("ang_done"), sem("pow_done")
        s1_done, k_prod, k_done, kj_done = sem("s1_done"), sem("k_prod"), sem("k_done"), sem("kj_done")
        bt_done, bt_turned, btT_done = sem("bt_done"), sem("bt_turned"), sem("btT_done")
        s2_done, tab_done, cos_done, sin_done = sem("s2_done"), sem("tab_done"), sem("cos_done"), sem("sin_done")
        kj_st = sem("kj_st")
        s1_st = sem("s1_st")
        s5_st = sem("s5_st")
        t_st = sem("t_st")
        x_in = sem("x_in")
        sw_in = [sem(f"sw_in{i}") for i in range(2)]
        sw_hi, sw_lo = sem("sw_hi"), sem("sw_lo")
        acc_full = sem("acc_full")
        acc_free = [sem(f"acc_free{i}") for i in range(ACC)]
        aux_full = sem("aux_full")
        aux_free = [sem(f"aux_free{i}") for i in range(AUX)]
        v_step, a_step = sem("v_step"), sem("a_step")
        sq_done, sum_done, suml_done = sem("sq_done"), sem("sum_done"), sem("suml_done")
        rec_done, rstd_done = sem("rec_done"), sem("rstd_done")
        nrm, nrm_hi, nrm_lo = sem("nrm"), sem("nrm_hi"), sem("nrm_lo")
        conv_done, gates_done, q_done, sqrt_done = sem("conv_done"), sem("gates_done"), sem("q_done"), sem("sqrt_done")
        ylru_done = sem("ylru_done")
        z_st, u_in = [sem(f"z_st{i}") for i in range(KL)], [sem(f"u_in{i}") for i in range(KL)]
        ring_in = [sem(f"ring_in{i}") for i in range(4)]
        data0_done, p_done = sem("data0_done"), sem("p_done")
        g_st, ys_in = sem("g_st"), sem("ys_in")
        g_hi, g_lo, yssm_done = sem("g_hi"), sem("g_lo"), sem("yssm_done")
        fr_in = [sem(f"fr_in{i}") for i in range(2)]
        gu_hi, gu_lo, dn_hi, dn_lo = sem("gu_hi"), sem("gu_lo"), sem("dn_hi"), sem("dn_lo")
        silu_done, f_done, ff_hi, ff_lo = sem("silu_done"), sem("f_done"), sem("ff_hi"), sem("ff_lo")
        y_done, st_out = sem("y_done"), sem("st_out")
        y_st = [sem(f"y_st{k}") for k in range(KD)]

        block = ctx.enter_context(nc.Block())

        def acc_n(b, key):
            return b * ACC_BLOCK + ACC_AT[key]

        def aux_n(b, key):
            return b * AUX_BLOCK + AUX_AT[key]

        def wait_acc(eng, b, key):
            eng.wait_ge(acc_full, acc_n(b, key) + 1)
            return acc_n(b, key) % ACC

        def wait_aux(eng, b, key):
            eng.wait_ge(aux_full, aux_n(b, key) + 1)
            return aux_n(b, key) % AUX

        def wait_evacuated(eng, b, key):
            eng.wait_ge(acc_free[acc_n(b, key) % ACC], acc_n(b, key) // ACC + 1)

        LASTP = NPC - 1

        def wait_chunk_used(eng, n):
            b, w = divmod(n, NSMALL)
            key = IN_ORDER[w] if w < 12 else ("glu", w - 12) if w < 12 + KL else ("out", w - 12 - KL)
            eng.wait_ge(acc_full, acc_n(b, (*key, LASTP)) + 1)

        def chunk_size(n):
            return KL * P if 12 <= n % NSMALL < 12 + KL else KD * P

        def ffn_acc(b, i, m):
            return i * (4 * NPC) + (b * ACC_BLOCK + ACC_MIX + m)

        def ffn_acc_uses(b, i, m):
            return i * (4 * NPC // ACC) + ((b * ACC_BLOCK + ACC_MIX) // ACC + m // ACC)

        def ffn_aux(b, i, m):
            return i * (KD * NPC) + (b * AUX_BLOCK + AUX_MIX + m)

        def ffn_aux_uses(b, i, m):
            return i * (KD * NPC // AUX) + (b * AUX_BLOCK + AUX_MIX + m) // AUX

        def chunk(b, i, q):
            return i * 2 + (b * NF + q)

        def sq_at(b, which):
            return b * before(None, n_sq) + before(which, n_sq)

        def sum_at(b, which):
            return b * before(None, n_sum) + before(which, n_sum)

        def nrm_at(b, which):
            return b * before(None, n_nrm) + before(which, n_nrm)

        def norm_n(b, which):
            return b * len(NORMS) + NORMS.index(which)

        params = ((p5[:], "p5"), (kf[:], "kf"), (bc[:], "bc"), (jrow[:], "jrow"), (dsk[:], "dsk"),
                  (ident[:], "ident"), (swap[:], "swap"), (lmask[:], "lmask"), (w_gates[:], "w_gates"),
                  (vec[:], "vec"), (small[:, SGN:SGN + 1], "sgn"), (carry5[:], "carry5"),
                  (conv_st[:], "conv_st"), (lru_st[:], "lru_st"))
        N_S5ST = 5

        @block.sync
        def _(sp):
            for dst, name in params:
                sp.dma_start(dst, a[name]).then_inc(par_in, 16)

            def load_small(n):
                if n >= 2:
                    sp.wait_ge(sw_lo, n - 1)
                w = n % NSMALL
                src = a["w_in"][w] if w < 12 else a["w_glu"][w - 12] if w < 12 + KL else a["w_out"][w - 12 - KL]
                sp.dma_start(sw_raw[:, n % 2, 0:chunk_size(n)], src).then_inc(sw_in[n % 2], 16)

            for k in range(KD):
                sp.dma_start(x_acc[:, k, :], a["x"][0][:, k, :]).then_inc(x_in, 16)
            for b in range(BLOCKS):
                for w in range(14):
                    load_small(b * NSMALL + w)
                    if b == 0 and w == 1:
                        sp.wait_ge(kj_st, 32)
                        for s in range(L):
                            sp.dma_start(s5_dram[s * HG:(s + 1) * HG, :, 4 * P:5 * P],
                                         k_dram[:, :, (7 - s) * HG:(7 - s) * HG + P]).then_inc(t_st, 16)
                wait_chunk_used(sp, b * NSMALL + 11)
                if b == 0:
                    sp.wait_ge(s1_st, 16)
                    sp.wait_ge(s5_st, 16 * N_S5ST)
                    sp.wait_ge(t_st, 16 * L)
                for t in range(GP):
                    if t % 4 == 0:
                        sp.wait_ge(z_st[t // 4], 16 * GE * (b + 1))
                        sp.dma_start(u5[:, 2 * t:2 * t + 8, :],
                                     z_dram[b].rearrange("s h g c -> (s h) g c")[:, 2 * t:2 * t + 8, :])\
                          .then_inc(u_in[t // 4], 16)
                    if t >= 4:
                        wait_acc(sp, b, ("y5", t - 4, 0))
                    sp.dma_start(s5ring[:, t % 4, :, :], s5_dram[:, 2 * t:2 * t + 2, :]).then_inc(ring_in[t % 4], 16)
                for w in range(14, NSMALL):
                    load_small(b * NSMALL + w)
                    if w == NSMALL - 4:
                        wait_acc(sp, b, ("glu", KL - 1, LASTP))
                        for q in range(2):
                            sp.dma_start(f_raw[:, q, :], a["w_ffn"][q]).then_inc(fr_in[q], 16)
                with sp.Fori(0, NI - 1) as i:
                    for q in range(2):
                        sp.wait_ge(gu_lo, chunk(b, i, q) + 1)
                        sp.wait_ge(dn_lo, chunk(b, i, q) + 1)
                        src = a["w_ffn"][bass.ds(i * 2 + (2 + q), 1)].rearrange("a p n -> (a p) n")
                        sp.dma_start(f_raw[:, q, :], src).then_inc(fr_in[q], 16)
                if b + 1 < BLOCKS:
                    for k in range(KD):
                        sp.wait_ge(y_st[k], 16 * (b + 1))
                        sp.dma_start(x_acc[:, k, :], a["x"][b + 1][:, k, :]).then_inc(x_in, 16)

        @block.gpsimd
        def _(po):
            po.memset(ones[:], 1.0).then_inc(consts, 1)
            po.memset(small[:, HPI:HPI + 1], math.pi / 2).then_inc(consts, 1)
            po.memset(zero[:], 0.0).then_inc(consts, 1)
            po.wait_ge(consts, 3)
            po.dma_start(k_dram[:, :, 0:7 * HG], zero[:]).then_inc(kj_st, 16)
            po.wait_ge(s1_done, 1)
            po.dma_start(s5_dram[:, :, 2 * P:3 * P], bt[1][:, :, 1:9, :].rearrange("p g t h -> p g (t h)"))\
              .then_inc(s1_st, 16)
            po.wait_ge(kj_done, 1)
            po.dma_start(k_dram[:, :, 7 * HG:15 * HG], kj[:].rearrange("h g j c -> h g (j c)")).then_inc(kj_st, 16)
            po.wait_ge(btT_done, 8)
            po.dma_start(s5_dram[:, :, 0:P], btT[:]).then_inc(s5_st, 16)
            po.wait_ge(btT_done, 16)
            po.dma_start(s5_dram[:, :, P:2 * P], btT[:]).then_inc(s5_st, 16)
            po.wait_ge(s2_done, 1)
            po.dma_start(s5_dram[:, :, 3 * P:4 * P], bt[1][:, :, 1:9, :].rearrange("p g t h -> p g (t h)"))\
              .then_inc(s5_st, 16)
            po.wait_ge(cos_done, 1)
            po.dma_start(s5_dram[:, :, 5 * P:5 * P + NW], tb[1][:]).then_inc(s5_st, 16)
            po.wait_ge(sin_done, 1)
            po.dma_start(s5_dram[:, :, 5 * P + NW:SP5], tb[2][:]).then_inc(s5_st, 16)

            for b in range(BLOCKS):
                for e in range(KL):
                    for p in range(NPC):
                        wait_evacuated(po, b, ("us", e, p))
                    for gl in range(GE):
                        po.dma_start(z_dram[b][:, :, e * GE + gl, :].rearrange("s h c -> h s c"),
                                     zs[gl * HG:(gl + 1) * HG, e, :, :]).then_inc(z_st[e], 16)
                po.wait_ge(ylru_done, KL * (b + 1))
                for t in range(GP):
                    if t >= 2:
                        po.wait_ge(p_done, b * GP + t - 1)
                    for q in range(2):
                        po.tensor_scalar(s5tmp[:, t % 2, 6, q, :], lmask[:], rho[:, 2 * t + q:2 * t + q + 1], None,
                                         ALU.mult).then_inc(data0_done, 1)
                    if t < KL:
                        po.tensor_tensor(tmp[:, 9 if t else 8, :], y_lru[:, t, :], y_lru[:, t, :], ALU.mult)\
                          .then_inc(suml_done, 1)
                        if t:
                            po.wait_ge(suml_done, (2 * KL - 1) * b + 2 * t)
                            po.tensor_tensor(tmp[:, 8, :], tmp[:, 8, :], tmp[:, 9, :], ALU.add).then_inc(suml_done, 1)
                            po.wait_ge(suml_done, (2 * KL - 1) * b + 2 * t + 1)
                wait_evacuated(po, b, ("y5", GP - 1, 0))
                po.dma_start(g_dram[b].rearrange("s h g c -> (s h) g c"), g5[:]).then_inc(g_st, 16)
                po.wait_ge(g_st, 16 * (b + 1))
                for e in range(KL):
                    po.wait_ge(z_st[e], 16 * GE * (b + 1))
                for gl in range(GE):
                    for e in range(KL):
                        po.dma_start(zs[gl * HG:(gl + 1) * HG, e, :, :],
                                     g_dram[b][:, :, e * GE + gl, :].rearrange("s h c -> h s c")).then_inc(ys_in, 16)
                for k in range(KD):
                    po.wait_ge(y_done, b * KD + k + 1)
                    po.dma_start(outs["y"][b][:, k, :], x_acc[:, k, :]).then_inc(y_st[k], 16)
            po.dma_start(outs["s5"], carry5[:]).then_inc(st_out, 16)
            po.dma_start(outs["conv"], conv_st[:]).then_inc(st_out, 16)
            po.dma_start(outs["lru"], lru_st[:]).then_inc(st_out, 16)
            po.wait_ge(st_out, 48)
            for k in range(KD):
                po.wait_ge(y_st[k], 16 * BLOCKS)

        @block.scalar
        def _(act):
            steps = [0]

            def link(ins):
                steps[0] += 1
                ins.then_inc(a_step, 1)
                act.wait_ge(a_step, steps[0])

            act.wait_ge(par_in, 16 * len(params))
            act.wait_ge(consts, 3)
            link(act.activation(pz[:, 16, 0:KL], vec[:, LAM:LAM + KL], ACT.Abs))
            act.activation(pz[:, 17, 0:KL], pz[:, 16, 0:KL], ACT.Exp, scale=-1.0)
            act.activation(pz[:, 0, :], p5[:, 2, :], ACT.Exp).then_inc(dt_done, 1)
            act.wait_ge(ang_done, 1)
            act.activation(rho[:], pz[:, 1, :], ACT.Exp, scale=float(L))
            link(act.activation(pt[2][:], pt[1][:], ACT.Exp))
            act.activation(pt[3][:], pt[0][:], ACT.Sin)
            link(act.activation(pt[1][:], pt[0][:], ACT.Abs))
            act.activation(pt[0][:], pt[1][:], ACT.Sin, bias=sm(HPI), scale=-1.0).then_inc(pow_done, 1)
            for n in range(16):
                act.wait_ge(bt_turned, n + 1)
                if n == 8:
                    act.wait_ge(s5_st, 16)
                act.activation(btT[:, 4 * (n % 8):4 * (n % 8) + 4, :].rearrange("p g c -> p (g c)"),
                               acc[:, (8 + n) % ACC, :], ACT.Copy).then_inc(btT_done, 1)
            act.wait_ge(tab_done, 1)
            link(act.activation(tb[2][:], tb[0][:], ACT.Abs))
            act.activation(tb[1][:], tb[2][:], ACT.Sin, bias=sm(HPI), scale=-TWO_PI).then_inc(cos_done, 1)
            act.wait_ge(cos_done, 1)
            act.activation(tb[2][:], tb[0][:], ACT.Sin, scale=sm(NS2PI)).then_inc(sin_done, 1)

            def small_hi(n):
                act.wait_ge(sw_in[n % 2], 16 * (n // 2 + 1))
                if n >= 2:
                    wait_chunk_used(act, n - 2)
                act.activation(sw_hl[:, n % 2, 0, 0:chunk_size(n)], sw_raw[:, n % 2, 0:chunk_size(n)],
                               ACT.Copy).then_inc(sw_hi, 1)

            def square(b, which, k, src, slots):
                if k >= 2:
                    act.wait_ge(sum_done, sum_at(b, which) + max(1, k - 2))
                act.activation(slots[k % 2], src, ACT.Square).then_inc(sq_done, 1)

            def rsqrt(b, which, dst):
                act.wait_ge(rec_done, norm_n(b, which) + 1)
                act.activation(dst, dst, ACT.Sqrt).then_inc(rstd_done, 1)

            def norm_hi(b, which, k, src, dst):
                act.wait_ge(nrm, nrm_at(b, which) + k + 1)
                act.activation(dst, src, ACT.Copy).then_inc(nrm_hi, 1)

            def pair_curves(b, j0):
                for j in (j0, j0 + 1):
                    wait_evacuated(act, b, ("r", j, LASTP))
                    act.activation(tmp[:, 2 + j % 2, :], tmp[:, 8 + j % 2, :], ACT.Tanh, scale=sm(CL + j))
                for j in (j0, j0 + 1):
                    act.activation(tmp[:, 4 + j % 2, :], tmp[:, 8 + j % 2, :], ACT.Exp, scale=sm(NCL + j))
                    act.activation(tmp[:, 8 + j % 2, :], tmp[:, 8 + j % 2, :], ACT.Exp, scale=sm(N2CL + j))\
                       .then_inc(gates_done, 1)

            def pair_sqrt(b, j0):
                for j in (j0, j0 + 1):
                    act.wait_ge(q_done, b * KL + j + 1)
                    act.activation(tmp[:, 2 + j % 2, :], tmp[:, 2 + j % 2, :], ACT.Sqrt).then_inc(sqrt_done, 1)

            def gu_split(b, i, q):
                act.wait_ge(fr_in[q], i * 16 + 16 * (b * NI + 1))
                act.activation(gu_hl[:, q, 0, :], f_raw[:, q, 0:2 * D], ACT.Copy).then_inc(gu_hi, 1)

            def ffn(b, i, last):
                act.wait_ge(aux_full, ffn_aux(b, i, 0))
                for q in range(2):
                    act.activation(dn_hl[:, q, 0, :], f_raw[:, q, 2 * D:3 * D], ACT.Copy).then_inc(dn_hi, 1)
                for q in range(2):
                    def hidden_hi(p):
                        t0, n = PIECES[p]
                        m = q * 2 * NPC + 2 * p + 1
                        act.wait_ge(acc_free[m % ACC], ffn_acc_uses(b, i, m) + 1)
                        act.activation(ff_hl[:, q, 0, t0:t0 + n], f_tmp[:, 3 + p, 0:n], ACT.Copy).then_inc(ff_hi, 1)

                    for p, (t0, n) in enumerate(PIECES):
                        m = q * 2 * NPC + 2 * p
                        act.wait_ge(acc_full, ffn_acc(b, i, m + 1))
                        act.activation(f_tmp[:, p, 0:n], acc[:, m % ACC, 0:n], ACT.Silu).then_inc(acc_free[m % ACC], 1)
                        if p:
                            hidden_hi(p - 1)
                    hidden_hi(NPC - 1)
                    if not last:
                        act.wait_ge(acc_full, ffn_acc(b, i, (q + 1) * 2 * NPC))
                        gu_split(b, i + 1, q)

            def natural(ap):
                return ap.rearrange("p s c -> p c s")

            def tokens(ap):
                return ap.rearrange("p (c s) -> p c s", s=L)

            for b in range(BLOCKS):
                w0 = b * NSMALL
                act.wait_ge(x_in, 16 * KD * (b + 1))
                if b == 0:
                    act.wait_ge(s5_st, 16 * N_S5ST)
                for k in range(KD):
                    square(b, "n1", k, x_acc[:, k, :], [tmp[:, 0, :], tmp[:, 1, :]])
                small_hi(w0)
                small_hi(w0 + 1)
                rsqrt(b, "n1", tmp[:, 3, :])
                for k in range(KD):
                    norm_hi(b, "n1", k, tmp[:, 4 + k % 2, :], act_hl[:, 0, k, :])
                for kind, j in PHASE1:
                    if kind == "gate":
                        for p, (t0, n) in enumerate(PIECES):
                            for g, slot, bias in (("r", 8, B_A), ("ig", 0, B_X)):
                                bank = wait_acc(act, b, (g, j, p))
                                if j >= 2:
                                    act.wait_ge(ylru_done, b * KL + j - 1)
                                act.activation(tmp[:, slot + j % 2, t0:t0 + n], acc[:, bank, 0:n], ACT.Sigmoid,
                                               bias=v1(bias + j)).then_inc(acc_free[bank], 1)
                        if j % 2:
                            pair_curves(b, j - 1)
                        if j == 3:
                            pair_sqrt(b, 2)
                        continue
                    for p, (t0, n) in enumerate(PIECES):
                        if kind == "xl":
                            continue
                        bank = wait_acc(act, b, (kind, j, p))
                        if kind == "us":
                            act.activation(zs[:, j, :, t0 // L:(t0 + n) // L],
                                           acc[:, bank, 0:n].rearrange("p (c s) -> p s c", s=L), ACT.Copy)\
                               .then_inc(acc_free[bank], 1)
                        else:
                            act.activation(y_lru[:, j, t0:t0 + n], acc[:, bank, 0:n], ACT.Gelu_apprx_tanh)\
                               .then_inc(acc_free[bank], 1)
                    w = IN_ORDER.index((kind, j))
                    small_hi(w0 + w + 2)
                    if (kind, j) == ("xl", 2):
                        pair_sqrt(b, 0)
                for t in range(GP):
                    bank = wait_acc(act, b, ("y5", t, 0))
                    act.activation(g5[:, 2 * t:2 * t + 2, :].rearrange("p q c -> p (q c)"), acc[:, bank, 0:2 * NC],
                                   ACT.Gelu_apprx_tanh).then_inc(acc_free[bank], 1)
                rsqrt(b, "nl", tmp[:, 8, :])
                for j in range(KL):
                    norm_hi(b, "nl", j, y_lru[:, j, :], act_hl[:, 0, j, :])
                act.wait_ge(ys_in, 16 * G * (b + 1))
                for j in range(KL):
                    act.activation(tokens(g_hl[:, 0, j, :]), natural(zs[:, j, :, :]), ACT.Copy).then_inc(g_hi, 1)
                for j in range(KL):
                    sig = btmp[:, 3, :] if j % 2 == 0 else sig2[:]
                    for p, (t0, n) in enumerate(PIECES):
                        bank = wait_acc(act, b, ("glu", j, p))
                        if j >= 2:
                            act.wait_ge(yssm_done, b * KL + j - 1)
                        act.activation(sig.rearrange("p (s c) -> p s c", s=L)[:, :, t0 // L:(t0 + n) // L],
                                       acc[:, bank, 0:n].rearrange("p (c s) -> p s c", s=L), ACT.Sigmoid,
                                       bias=v1(B_GLU + j)).then_inc(acc_free[bank], 1)
                    small_hi(w0 + 12 + j + 2)
                    act.wait_ge(yssm_done, b * KL + j + 1)
                    square(b, "ns", j, zs[:, j, :, :].rearrange("p s c -> p (s c)"), [btmp[:, 0, :], btmp[:, 1, :]])
                rsqrt(b, "ns", tmp[:, 9, :])
                for j in range(KL):
                    norm_hi(b, "ns", j, natural(zs[:, j, :, :]), tokens(act_hl[:, 0, KL + j, :]))
                for d in range(KD):
                    if d + 2 < KD:
                        small_hi(w0 + 12 + KL + d + 2)
                    wait_evacuated(act, b, ("out", d, LASTP))
                    square(b, "n2", d, x_acc[:, d, :], [tmp[:, 8, :], tmp[:, 9, :]])
                for q in range(2):
                    gu_split(b, 0, q)
                rsqrt(b, "n2", tmp[:, 7, :])
                for k in range(KD):
                    norm_hi(b, "n2", k, h2_tmp[:, k % 2, :], act_hl[:, 0, k, :])
                with act.Fori(0, NI - 1) as i:
                    ffn(b, i, False)
                ffn(b, NI - 1, True)
                for m in range(KD * NPC - 2, KD * NPC):
                    bank = (b * AUX_BLOCK + AUX_MIX + m) % AUX
                    act.wait_ge(aux_free[bank], ffn_aux_uses(b, NI - 1, m) + 1)
                for k in range(KD):
                    square(b, "nf", k, x_acc[:, k, :], [tmp[:, 8, :], tmp[:, 9, :]])
                rsqrt(b, "nf", tmp[:, 7, :])

        @block.tensor
        def _(pe):
            pe.wait_ge(s1_done, 1)
            for c in range(8):
                if c >= ACC:
                    pe.wait_ge(k_done, c - ACC + 1)
                for g in range(4 * c, 4 * c + 4):
                    ins = pe.matmul(acc[0:HG, c % ACC, (g % 4) * P:(g % 4 + 1) * P], bb[:, 0, g, :],
                                    bt[1][:, g, 0:8, :].rearrange("p t h -> p (t h)"), start=True, stop=True)
                ins.then_inc(k_prod, 1)
            for n in range(16):
                pe.wait_ge(bt_done, n // 8 + 1)
                if 8 + n - ACC < 8:
                    pe.wait_ge(k_done, 8 + n - ACC + 1)
                else:
                    pe.wait_ge(btT_done, n - ACC + 1)
                for g in range(4 * (n % 8), 4 * (n % 8) + 4):
                    ins = pe.transpose(acc[:, (8 + n) % ACC, (g % 4) * P:(g % 4 + 1) * P],
                                       bt[0][:, g, 0:8, :].rearrange("p t h -> p (t h)"), ident[:])
                ins.then_inc(bt_turned, 1)
            pe.wait_ge(btT_done, 16)

            def three(out, w_hl, x_hl, first, last):
                pe.matmul(out, w_hl(0), x_hl(0), start=first, stop=False)
                pe.matmul(out, w_hl(0), x_hl(1), start=False, stop=False)
                return pe.matmul(out, w_hl(1), x_hl(0), start=False, stop=last)

            def acc_bank(b, key):
                bank, uses = acc_n(b, key) % ACC, acc_n(b, key) // ACC
                if uses:
                    pe.wait_ge(acc_free[bank], uses)
                return bank

            def aux_bank(b, key):
                bank, uses = aux_n(b, key) % AUX, aux_n(b, key) // AUX
                if uses:
                    pe.wait_ge(aux_free[bank], uses)
                return bank

            def sum_rows(b, which, src):
                for p, (t0, n) in enumerate(PIECES):
                    bank = aux_bank(b, (which, 0, p))
                    pe.matmul(aux[:, bank, 0:n], ones[:], src[:, t0:t0 + n], start=True, stop=True).then_inc(aux_full, 1)

            def small_product(b, w, key, kn, x_hl, ready=None):
                n = b * NSMALL + w
                pe.wait_ge(sw_lo, n + 1)
                for p, (t0, m) in enumerate(PIECES):
                    bank = acc_bank(b, (*key, p))
                    for k in range(kn):
                        if ready and p == 0:
                            ready(k)
                        ins = three(acc[:, bank, 0:m], lambda s: sw_hl[:, n % 2, s, k * P:(k + 1) * P],
                                    lambda s: x_hl[:, s, k, t0:t0 + m], k == 0, k == kn - 1)
                    ins.then_inc(acc_full, 1)

            def ffn(b, i):
                for q in range(2):
                    pe.wait_ge(gu_lo, chunk(b, i, q) + 1)
                    for p, (t0, n) in enumerate(PIECES):
                        for u in range(2):
                            m = q * 2 * NPC + 2 * p + u
                            pe.wait_ge(acc_free[m % ACC], ffn_acc_uses(b, i, m))
                            for k in range(KD):
                                c = (u * KD + k) * P
                                ins = three(acc[:, m % ACC, 0:n], lambda s: gu_hl[:, q, s, c:c + P],
                                            lambda s: act_hl[:, s, k, t0:t0 + n], k == 0, k == KD - 1)
                            ins.then_inc(acc_full, 1)
                pe.wait_ge(dn_lo, chunk(b, i, 1) + 1)
                for p, (t0, n) in enumerate(PIECES):
                    pe.wait_ge(ff_lo, i * (2 * NPC) + (b * NI * 2 * NPC + NPC + p + 1))
                    for d in range(KD):
                        m = p * KD + d
                        bank = (b * AUX_BLOCK + AUX_MIX + m) % AUX
                        pe.wait_ge(aux_free[bank], ffn_aux_uses(b, i, m))
                        for q in range(2):
                            ins = three(aux[:, bank, 0:n], lambda s: dn_hl[:, q, s, d * P:(d + 1) * P],
                                        lambda s: ff_hl[:, q, s, t0:t0 + n], q == 0, q == 1)
                        ins.then_inc(aux_full, 1)

            for b in range(BLOCKS):
                pe.wait_ge(sum_done, sum_at(b, "n1") + KD - 1)
                sum_rows(b, "n1", tmp[:, 2, :])
                for kind, j in PHASE1:
                    if kind == "gate":
                        pe.wait_ge(conv_done, b * KL + j + 1)
                        for p, (t0, n) in enumerate(PIECES):
                            for g, name in enumerate(("r", "ig")):
                                bank = acc_bank(b, (name, j, p))
                                pe.matmul(acc[:, bank, 0:n], w_gates[:, g, j, :], tmp[:, 6 + j % 2, t0:t0 + n],
                                          start=True, stop=True).then_inc(acc_full, 1)
                    else:
                        w = IN_ORDER.index((kind, j))
                        small_product(b, w, (kind, j), KD, act_hl,
                                      (lambda k: pe.wait_ge(nrm_lo, nrm_at(b, "n1") + k + 1)) if w == 0 else None)
                for t in range(GP + 2):
                    if t >= 2:
                        o = t - 2
                        pe.wait_ge(p_done, b * GP + o + 1)
                        bank = acc_bank(b, ("y5", o, 0))
                        for q in range(2):
                            g, out = 2 * o + q, acc[:, bank, q * NC:(q + 1) * NC]
                            par = s5ring[:, o % 4, q, :]
                            pe.matmul(out, par[:, 4 * P:5 * P], u5[:, g, :], start=True, stop=False)
                            pe.matmul(out, par[:, 2 * P:3 * P], s5tmp[:, o % 2, 4, q, 0:NC], start=False, stop=False)
                            ins = pe.matmul(out, par[:, 3 * P:4 * P], s5tmp[:, o % 2, 5, q, 0:NC], start=False, stop=True)
                        ins.then_inc(acc_full, 1)
                    if t < GP:
                        pe.wait_ge(u_in[t // 4], 16 * (b + 1))
                        pe.wait_ge(ring_in[t % 4], 16 * (b * 4 + t // 4 + 1))
                        for v in range(2):
                            bank = acc_bank(b, (("v1", "v2")[v], t, 0))
                            for q in range(2):
                                ins = pe.matmul(acc[:, bank, q * NC:(q + 1) * NC], s5ring[:, t % 4, q, v * P:(v + 1) * P],
                                                u5[:, 2 * t + q, :], start=True, stop=True)
                            ins.then_inc(acc_full, 1)
                bank = aux_bank(b, ("fin", 0, 0))
                pe.matmul(aux[:, bank, 0:2 * G], ident[:], fin5[:, 0].rearrange("p g s -> p (g s)"), start=True, stop=False)
                pe.matmul(aux[:, bank, 0:2 * G], swap[:], fin5[:, 1].rearrange("p g s -> p (g s)"), start=False,
                          stop=True).then_inc(aux_full, 1)
                pe.wait_ge(suml_done, (2 * KL - 1) * (b + 1))
                sum_rows(b, "nl", tmp[:, 8, :])
                for j in range(KL):
                    small_product(b, 12 + j, ("glu", j), KL, g_hl,
                                  (lambda k: pe.wait_ge(g_lo, b * KL + k + 1)) if j == 0 else None)
                pe.wait_ge(sum_done, sum_at(b, "ns") + KL - 1)
                sum_rows(b, "ns", btmp[:, 2, :])
                for d in range(KD):
                    small_product(b, 12 + KL + d, ("out", d), KD, act_hl,
                                  (lambda k: pe.wait_ge(nrm_lo, nrm_at(b, "nl") + k + 1)) if d == 0 else None)
                pe.wait_ge(sum_done, sum_at(b, "n2") + KD - 1)
                sum_rows(b, "n2", tmp[:, 6, :])
                pe.wait_ge(nrm_lo, nrm_at(b, "n2") + KD)
                with pe.Fori(0, NI - 1) as i:
                    ffn(b, i)
                ffn(b, NI - 1)
                pe.wait_ge(sum_done, sum_at(b, "nf") + KD - 1)
                sum_rows(b, "nf", tmp[:, 6, :])

        @block.vector
        def _(v):
            steps = [0]

            def link(ins):
                steps[0] += 1
                ins.then_inc(v_step, 1)
                v.wait_ge(v_step, steps[0])

            def tt(out, x, y, op):
                return v.tensor_tensor(out, x, y, op)

            def stt(out, x, s, y, op0, op1):
                return v.scalar_tensor_tensor(out=out, in0=x, scalar=s, in1=y, op0=op0, op1=op1)

            MUL, ADD, SUB = ALU.mult, ALU.add, ALU.subtract

            def turn_down(x, n):
                link(v.tensor_scalar(n, x, 1.0 / TWO_PI, MAGIC, MUL, ADD))
                link(v.tensor_scalar(n, n, MAGIC, None, SUB))
                for part in (PI_A, PI_B, PI_C):
                    link(stt(x, n, -part, x, MUL, ADD))
                link(v.tensor_scalar(x, x, 3.1415925, -3.1415925, ALU.min, ALU.max))

            def z(n):
                return pz[:, n, :]

            v.wait_ge(dt_done, 1)
            link(tt(z(1), p5[:, 0, :], z(0), MUL))
            link(tt(z(4), p5[:, 1, :], z(0), MUL))
            turn_down(z(4), z(3))
            link(tt(pt[0][:], z(4).unsqueeze(2).broadcast_to([P, G, NPOW]),
                    kf[:].unsqueeze(1).broadcast_to([P, G, NPOW]), MUL))
            turn_down(pt[0][:], pt[2][:])
            tt(pt[1][:], z(1).unsqueeze(2).broadcast_to([P, G, NPOW]),
               kf[:].unsqueeze(1).broadcast_to([P, G, NPOW]), MUL).then_inc(ang_done, 1)
            e, t2, w2, po_ = (pz[:, n, 0:KL] for n in (17, 18, 19, 16))
            lam = vec[:, LAM:LAM + KL]
            link(v.tensor_scalar(t2, e, 2.0, None, ADD))
            link(v.reciprocal(w2, t2))
            link(tt(e, e, w2, MUL))
            link(tt(w2, e, e, MUL))
            link(v.tensor_scalar(po_, w2, 1.0 / (2 * LN_TERMS - 1), 1.0 / (2 * LN_TERMS - 3), MUL, ADD))
            for m in range(LN_TERMS - 3, -1, -1):
                link(tt(po_, po_, w2, MUL))
                link(v.tensor_scalar(po_, po_, 1.0 / (2 * m + 1), None, ADD))
            link(tt(po_, po_, e, MUL))
            link(v.tensor_scalar(t2, lam, -1.0, 0.0, MUL, ALU.max))
            link(stt(t2, po_, 2.0, t2, MUL, ADD))
            v.tensor_scalar(small[:, CL:CL + KL], t2, LRU_C, None, MUL)
            v.tensor_scalar(small[:, NCL:NCL + KL], t2, -LRU_C, None, MUL)
            v.tensor_scalar(small[:, N2CL:N2CL + KL], t2, -2.0 * LRU_C, None, MUL)
            link(v.tensor_scalar(sm(NS2PI), sm(SGN), -TWO_PI, None, MUL))
            link(v.tensor_scalar(tau[:, 0, :], z(4), L / TWO_PI, None, MUL))
            link(v.tensor_scalar(z(3), tau[:, 0, :], MAGIC, None, ADD))
            link(v.tensor_scalar(z(3), z(3), MAGIC, None, SUB))
            link(tt(tau[:, 0, :], tau[:, 0, :], z(3), SUB))
            link(v.tensor_scalar(z(3), tau[:, 0, :], MAGIC12, None, ADD))
            link(v.tensor_scalar(tau[:, 1, :], z(3), MAGIC12, None, SUB))
            link(tt(tau[:, 2, :], tau[:, 0, :], tau[:, 1, :], SUB))
            v.wait_ge(pow_done, 1)
            tt(pw[:, 0], pt[2][:], pt[0][:], MUL)
            link(tt(pw[:, 1], pt[2][:], pt[3][:], MUL))
            link(v.tensor_scalar(pw[:, 2], pw[:, 1], sm(SGN), None, MUL))
            lr, li = p5[:, 0, :], p5[:, 1, :]
            ni = z(6)
            v.tensor_copy(ni, pw[:, 1, :, 9])
            v.tensor_scalar(z(5), pw[:, 0, :, 9], 1.0, None, SUB)
            tt(z(7), lr, lr, MUL)
            link(tt(z(8), li, li, MUL))
            link(tt(z(7), z(7), z(8), ADD))
            link(v.reciprocal(z(7), z(7)))
            tt(z(8), z(5), lr, MUL)
            link(tt(z(9), ni, li, MUL))
            link(tt(z(8), z(8), z(9), ADD))
            link(tt(z(8), z(8), z(7), MUL))
            tt(z(9), ni, lr, MUL)
            link(tt(z(10), z(5), li, MUL))
            link(tt(z(9), z(9), z(10), SUB))
            link(tt(z(9), z(9), z(7), MUL))
            link(v.tensor_scalar(z(9), z(9), sm(SGN), None, MUL))

            def gh(x):
                return x.unsqueeze(2).broadcast_to([P, G, HG])

            tt(bb[:, 0], bc[:, 0], gh(z(8)), MUL)
            link(tt(bb[:, 2], bc[:, 1], gh(z(9)), MUL))
            tt(bb[:, 1], bc[:, 1], gh(z(8)), MUL)
            link(tt(bb[:, 3], bc[:, 0], gh(z(9)), MUL))
            link(tt(bb[:, 0], bb[:, 0], bb[:, 2], ADD))
            link(tt(bb[:, 1], bb[:, 1], bb[:, 3], SUB))
            link(v.tensor_scalar(bb[:, 2], bc[:, 2], sm(SGN), -1.0, MUL, MUL))
            link(v.tensor_scalar(bb[:, 3], bc[:, 3], sm(SGN), None, MUL))

            def powers(x, r, k0, kn):
                return (x.unsqueeze(2).broadcast_to([P, G, kn, HG]),
                        pw[:, r, :, k0:k0 + kn].unsqueeze(3).broadcast_to([P, G, kn, HG]))

            tt(bt[1][:], *powers(bb[:, 2], 0, 8, 9), MUL)
            link(tt(bt[0][:], *powers(bc[:, 3], 1, 8, 9), MUL))
            tt(bt[1][:], bt[1][:], bt[0][:], SUB).then_inc(s1_done, 1)
            tt(dd[:], ident[0:HG, 0:HG].unsqueeze(1).broadcast_to([HG, G, HG]),
               dsk[:].unsqueeze(2).broadcast_to([HG, G, HG]), MUL)
            for c in range(8):
                v.wait_ge(k_prod, c + 1)
                v.tensor_copy(kj[:, 4 * c:4 * c + 4].rearrange("p g j h -> p (g j h)"), acc[0:HG, c % ACC, :])\
                 .then_inc(k_done, 1)
            v.wait_ge(k_done, 8)
            tt(kj[:, :, 0, :], kj[:, :, 0, :], dd[:], ADD).then_inc(kj_done, 1)
            v.wait_ge(s1_st, 16)
            for m, (x, y, op) in enumerate(((0, 1, ADD), (1, 0, SUB))):
                if m:
                    v.wait_ge(bt_turned, 8)
                tt(bt[0][:, :, 0:8], *powers(bb[:, x], 0, 0, 8), MUL)
                link(tt(bt[1][:, :, 0:8], *powers(bb[:, y], 2, 0, 8), MUL))
                tt(bt[0][:, :, 0:8], bt[0][:, :, 0:8], bt[1][:, :, 0:8], op).then_inc(bt_done, 1)
            v.wait_ge(bt_turned, 16)
            tt(bt[1][:, :, 1:9], *powers(bb[:, 3], 0, 9, 8), MUL)
            link(tt(bt[0][:, :, 1:9], *powers(bc[:, 2], 1, 9, 8), MUL))
            tt(bt[1][:, :, 1:9], bt[1][:, :, 1:9], bt[0][:, :, 1:9], SUB).then_inc(s2_done, 1)
            jb = jrow[:].unsqueeze(1).broadcast_to([P, G, NW])
            v.wait_ge(kj_st, 32)
            tt(tb[0][:], jb, tau[:, 1, :].unsqueeze(2).broadcast_to([P, G, NW]), MUL)
            link(tt(tb[1][:], jb, tau[:, 2, :].unsqueeze(2).broadcast_to([P, G, NW]), MUL))
            link(tt(tb[2][:], tb[0][:], tb[1][:], ADD))
            link(v.tensor_scalar(tb[2][:], tb[2][:], MAGIC, None, ADD))
            link(v.tensor_scalar(tb[2][:], tb[2][:], MAGIC, None, SUB))
            link(tt(tb[0][:], tb[0][:], tb[2][:], SUB))
            link(tt(tb[0][:], tb[0][:], tb[1][:], ADD))
            v.tensor_scalar(tb[0][:], tb[0][:], 0.49999997, -0.49999997, ALU.min, ALU.max).then_inc(tab_done, 1)

            def small_lo(n):
                v.wait_ge(sw_hi, n + 1)
                c = chunk_size(n)
                tt(sw_hl[:, n % 2, 1, 0:c], sw_raw[:, n % 2, 0:c], sw_hl[:, n % 2, 0, 0:c].bitcast(F32), SUB)\
                    .then_inc(sw_lo, 1)

            def sum_up(b, which, m, slots, dst):
                v.wait_ge(sq_done, sq_at(b, which) + m + 1)
                if m > 1:
                    v.wait_ge(sum_done, sum_at(b, which) + m - 1)
                tt(dst, slots[0] if m == 1 else dst, slots[m % 2], ADD).then_inc(sum_done, 1)

            def reciprocal_mean(b, which, width, dst):
                for p, (t0, n) in enumerate(PIECES):
                    bank = wait_aux(v, b, (which, 0, p))
                    v.tensor_scalar(dst[:, t0:t0 + n], aux[:, bank, 0:n], 1.0 / width, EPS, MUL, ADD)\
                     .then_inc(aux_free[bank], 1)
                v.wait_ge(aux_free[bank], aux_n(b, (which, 0, LASTP)) // AUX + 1)
                v.reciprocal(dst, dst).then_inc(rec_done, 1)

            def norm(b, which, gain, rstd, src, dst, lo_src, out):
                n = NCH[which]
                v.wait_ge(rstd_done, norm_n(b, which) + 1)
                for k in range(n + 1):
                    if k < n:
                        if k >= 2:
                            v.wait_ge(nrm_lo, nrm_at(b, which) + k - 1)
                        stt(dst(k), src(k), v1(gain + k), rstd, MUL, MUL).then_inc(nrm, 1)
                    if k:
                        v.wait_ge(nrm_hi, nrm_at(b, which) + k)
                        hi, lo = out(k - 1)
                        tt(lo, lo_src(k - 1), hi, SUB).then_inc(nrm_lo, 1)

            def natural(ap):
                return ap.rearrange("p s c -> p c s")

            def tokens(ap):
                return ap.rearrange("p (c s) -> p c s", s=L)

            def flat(ap):
                return ap.rearrange("p s c -> p (s c)")

            def lru_inputs(b, j):
                if b or j:
                    v.wait_ge(conv_done, b * KL + j)
                for p, (t0, n) in enumerate(PIECES):
                    bank = wait_acc(v, b, ("xl", j, p))
                    v.tensor_copy(xl[:, 3 + t0:3 + t0 + n], acc[:, bank, 0:n]).then_inc(acc_free[bank], 1)
                wait_evacuated(v, b, ("xl", j, LASTP))
                v.tensor_copy(xl[:, 0:3], conv_st[:, j, 0, :])
                link(v.tensor_copy(xl[:, S0:S0 + 3], conv_st[:, j, 1, :]))
                v.tensor_copy(conv_st[:, j, 0, :], xl[:, TP:TP + 3])
                v.tensor_copy(conv_st[:, j, 1, :], xl[:, TB:TB + 3])
                xc = tmp[:, 6 + j % 2, :]
                link(v.tensor_scalar(xc, xl[:, 0:TB], v1(CONV + j), v1(CONVB + j), MUL, ADD))
                for k in range(1, CONV_W):
                    ins = stt(xc, xl[:, k:k + TB], v1(CONV + KL * k + j), xc, MUL, ADD)
                    if k < CONV_W - 1:
                        link(ins)
                ins.then_inc(conv_done, 1)

            def lru_bx(b, j):
                wait_evacuated(v, b, ("ig", j, LASTP))
                v.wait_ge(conv_done, b * KL + j + 1)
                tt(tmp[:, j % 2, :], tmp[:, j % 2, :], tmp[:, 6 + j % 2, :], MUL)

            def lru_q(b, j):
                v.wait_ge(gates_done, b * KL + j + 1)
                stt(tmp[:, 2 + j % 2, :], tmp[:, 8 + j % 2, :], 1.0, tmp[:, 2 + j % 2, :], ADD, MUL).then_inc(q_done, 1)

            def lru_scan(b, j):
                v.wait_ge(sqrt_done, b * KL + j + 1)
                bx, h, decay = tmp[:, j % 2, :], tmp[:, 2 + j % 2, :], tmp[:, 4 + j % 2, :]
                link(tt(bx, bx, h, MUL))
                v.tensor_tensor_scan(h[:, 0:S0], decay[:, 0:S0], bx[:, 0:S0], lru_st[:, j, 0:1], MUL, ADD)
                link(v.tensor_tensor_scan(h[:, S0:TB], decay[:, S0:TB], bx[:, S0:TB], lru_st[:, j, 1:2], MUL, ADD))
                v.tensor_copy(lru_st[:, j, 0:1], h[:, TP - 1:TP])
                v.tensor_copy(lru_st[:, j, 1:2], h[:, TB - 1:TB])
                wait_evacuated(v, b, ("gl", j, LASTP))
                tt(y_lru[:, j, :], y_lru[:, j, :], h, MUL).then_inc(ylru_done, 1)

            def s5_states(b, t):
                s = s5tmp[:, t % 2]
                cos = s5ring[:, t % 4, :, 5 * P:5 * P + NW]
                sin = s5ring[:, t % 4, :, 5 * P + NW:SP5]
                v.wait_ge(ring_in[t % 4], 16 * (b * 4 + t // 4 + 1))
                for n, (key, tab) in enumerate((("v1", cos), ("v2", sin))):
                    bank = wait_acc(v, b, (key, t, 0))
                    tt(s[:, n, :, 0:NC], acc[:, bank, 0:2 * NC].rearrange("p (q c) -> p q c", q=2), tab[:, :, 1:NW],
                       MUL).then_inc(acc_free[bank], 1)
                wait_evacuated(v, b, ("v2", t, 0))
                link(tt(s[:, 2, :, 1:NW], s[:, 0, :, 0:NC], s[:, 1, :, 0:NC], ADD))
                link(v.tensor_copy(s[:, 2, :, 0:NW:CS], carry5[:, 2 * t:2 * t + 2, :]))
                v.wait_ge(data0_done, 2 * (b * GP + t + 1))
                link(v.tensor_tensor_scan(s[:, 3].rearrange("p q c -> p (q c)"), s[:, 6].rearrange("p q c -> p (q c)"),
                                          s[:, 2].rearrange("p q c -> p (q c)"), 0.0, MUL, ADD))
                if t >= 2:
                    wait_acc(v, b, ("y5", t - 2, 0))
                tt(s[:, 4], s[:, 3], cos, MUL)
                link(tt(s[:, 5], s[:, 3], sin, MUL))
                v.tensor_copy(fin5[:, 0, 2 * t:2 * t + 2, :], s[:, 4, :, CP:NW:CS - CP + NW - 1 - CS])
                v.tensor_copy(fin5[:, 1, 2 * t:2 * t + 2, :], s[:, 5, :, CP:NW:CS - CP + NW - 1 - CS]).then_inc(p_done, 1)

            def gu_lo_split(b, i, q):
                v.wait_ge(gu_hi, chunk(b, i, q) + 1)
                tt(gu_hl[:, q, 1, :], f_raw[:, q, 0:2 * D], gu_hl[:, q, 0, :].bitcast(F32), SUB).then_inc(gu_lo, 1)

            def ffn(b, i, last):
                for q in range(2):
                    v.wait_ge(dn_hi, chunk(b, i, q) + 1)
                    tt(dn_hl[:, q, 1, :], f_raw[:, q, 2 * D:3 * D], dn_hl[:, q, 0, :].bitcast(F32), SUB).then_inc(dn_lo, 1)
                for q in range(2):
                    def hidden_lo(p):
                        t0, n = PIECES[p]
                        v.wait_ge(ff_hi, i * (2 * NPC) + (b * NI * 2 * NPC + q * NPC + p + 1))
                        tt(ff_hl[:, q, 1, t0:t0 + n], f_tmp[:, 3 + p, 0:n], ff_hl[:, q, 0, t0:t0 + n].bitcast(F32), SUB)\
                            .then_inc(ff_lo, 1)

                    for p, (t0, n) in enumerate(PIECES):
                        m = q * 2 * NPC + 2 * p
                        v.wait_ge(acc_free[m % ACC], ffn_acc_uses(b, i, m) + 1)
                        v.wait_ge(acc_full, ffn_acc(b, i, m + 2))
                        if q:
                            v.wait_ge(ff_lo, i * (2 * NPC) + (b * NI * 2 * NPC + p + 1))
                        tt(f_tmp[:, 3 + p, 0:n], f_tmp[:, p, 0:n], acc[:, (m + 1) % ACC, 0:n], MUL)\
                            .then_inc(acc_free[(m + 1) % ACC], 1)
                        if p:
                            hidden_lo(p - 1)
                    hidden_lo(NPC - 1)
                    if not last:
                        gu_lo_split(b, i + 1, q)
                for p, (t0, n) in enumerate(PIECES):
                    for d in range(KD):
                        m = p * KD + d
                        bank = (b * AUX_BLOCK + AUX_MIX + m) % AUX
                        v.wait_ge(aux_full, ffn_aux(b, i, m + 1))
                        tt(x_acc[:, d, t0:t0 + n], x_acc[:, d, t0:t0 + n], aux[:, bank, 0:n], ADD).then_inc(aux_free[bank], 1)

            for b in range(BLOCKS):
                w0 = b * NSMALL
                for m in range(1, KD):
                    sum_up(b, "n1", m, [tmp[:, 0, :], tmp[:, 1, :]], tmp[:, 2, :])
                small_lo(w0)
                small_lo(w0 + 1)
                reciprocal_mean(b, "n1", D, tmp[:, 3, :])
                norm(b, "n1", G_MIX, tmp[:, 3, :], lambda k: x_acc[:, k, :], lambda k: tmp[:, 4 + k % 2, :],
                     lambda k: tmp[:, 4 + k % 2, :],
                     lambda k: (act_hl[:, 0, k, :].bitcast(F32), act_hl[:, 1, k, :]))
                for w, (kind, j) in enumerate(IN_ORDER):
                    if kind == "xl":
                        if j == 2:
                            lru_bx(b, 0)
                            lru_bx(b, 1)
                        lru_inputs(b, j)
                        if j == 2:
                            lru_q(b, 0)
                            lru_q(b, 1)
                    small_lo(w0 + w + 2)
                    if (kind, j) == ("xl", 3):
                        lru_scan(b, 0)
                        lru_scan(b, 1)
                for j in (2, 3):
                    lru_bx(b, j)
                for j in (2, 3):
                    lru_q(b, j)
                for j in (2, 3):
                    lru_scan(b, j)
                for t in range(GP):
                    s5_states(b, t)
                bank = wait_aux(v, b, ("fin", 0, 0))
                v.tensor_copy(carry5[:].rearrange("p g s -> p (g s)"), aux[:, bank, 0:2 * G]).then_inc(aux_free[bank], 1)
                reciprocal_mean(b, "nl", LRU_W, tmp[:, 8, :])
                wait_acc(v, b, ("y5", GP - 1, 0))
                norm(b, "nl", G_LRU, tmp[:, 8, :], lambda k: y_lru[:, k, :], lambda k: y_lru[:, k, :],
                     lambda k: y_lru[:, k, :], lambda k: (act_hl[:, 0, k, :].bitcast(F32), act_hl[:, 1, k, :]))
                for j in range(KL):
                    v.wait_ge(g_hi, b * KL + j + 1)
                    tt(tokens(g_hl[:, 1, j, :]), natural(zs[:, j]), tokens(g_hl[:, 0, j, :].bitcast(F32)), SUB)\
                        .then_inc(g_lo, 1)
                for j in range(KL):
                    wait_evacuated(v, b, ("glu", j, LASTP))
                    sig = btmp[:, 3, :] if j % 2 == 0 else sig2[:]
                    tt(flat(zs[:, j]), flat(zs[:, j]), sig, MUL).then_inc(yssm_done, 1)
                    small_lo(w0 + 12 + j + 2)
                    if j:
                        sum_up(b, "ns", j, [btmp[:, 0, :], btmp[:, 1, :]], btmp[:, 2, :])
                reciprocal_mean(b, "ns", SSM_W, tmp[:, 9, :])
                norm(b, "ns", G_SSM, tmp[:, 9, :], lambda k: flat(zs[:, k]), lambda k: flat(zs[:, k]),
                     lambda k: natural(zs[:, k]),
                     lambda k: (tokens(act_hl[:, 0, KL + k, :].bitcast(F32)), tokens(act_hl[:, 1, KL + k, :])))
                for d in range(KD):
                    if d + 2 < KD:
                        small_lo(w0 + 12 + KL + d + 2)
                    for p, (t0, n) in enumerate(PIECES):
                        bank = wait_acc(v, b, ("out", d, p))
                        tt(x_acc[:, d, t0:t0 + n], x_acc[:, d, t0:t0 + n], acc[:, bank, 0:n], ADD).then_inc(acc_free[bank], 1)
                    if d >= 2:
                        sum_up(b, "n2", d - 1, [tmp[:, 8, :], tmp[:, 9, :]], tmp[:, 6, :])
                sum_up(b, "n2", KD - 1, [tmp[:, 8, :], tmp[:, 9, :]], tmp[:, 6, :])
                for q in range(2):
                    gu_lo_split(b, 0, q)
                reciprocal_mean(b, "n2", D, tmp[:, 7, :])
                norm(b, "n2", G_FFN, tmp[:, 7, :], lambda k: x_acc[:, k, :], lambda k: h2_tmp[:, k % 2, :],
                     lambda k: h2_tmp[:, k % 2, :],
                     lambda k: (act_hl[:, 0, k, :].bitcast(F32), act_hl[:, 1, k, :]))
                with v.Fori(0, NI - 1) as i:
                    ffn(b, i, False)
                ffn(b, NI - 1, True)
                for m in range(1, KD):
                    sum_up(b, "nf", m, [tmp[:, 8, :], tmp[:, 9, :]], tmp[:, 6, :])
                reciprocal_mean(b, "nf", D, tmp[:, 7, :])
                v.wait_ge(rstd_done, norm_n(b, "nf") + 1)
                for k in range(KD):
                    stt(x_acc[:, k, :], x_acc[:, k, :], v1(G_FIN + k), tmp[:, 7, :], MUL, MUL).then_inc(y_done, 1)


def _layout(inp):
    import numpy as np

    f = {k: np.asarray(x)[0] if k not in ("x_prompt", "x_sample", "norm_final") else np.asarray(x)
         for k, x in inp.items()}
    out = {}
    xs = np.zeros((BLOCKS, TB, D), np.float32)
    for b in range(BLOCKS):
        xs[b, 0:TP] = f["x_prompt"][0, b * TP:(b + 1) * TP]
        xs[b, S0:TB] = f["x_sample"][0, b * TS:(b + 1) * TS]
    out["x"] = xs.reshape(BLOCKS, TB, KD, P).transpose(0, 3, 2, 1)

    def chunks(w):
        return w.reshape(w.shape[0] // P, P, w.shape[1] // P, P).transpose(2, 1, 0, 3).reshape(w.shape[1] // P, P, -1)

    at = {"xl": 0, "gl": KL, "us": 2 * KL}
    out["w_in"] = chunks(f["w_in"])[[at[k] + j for k, j in IN_ORDER]]
    out["w_glu"] = chunks(f["ssm_w_glu"])
    out["w_out"] = chunks(f["w_out"])
    out["w_ffn"] = np.concatenate([chunks(f["w_gate"]), chunks(f["w_up"]), f["w_down"].reshape(NF, P, D)], axis=2)

    def cols(x):
        return x.reshape(-1, P).T

    out["vec"] = np.concatenate([cols(f[k]) for k in ("norm_mix", "norm_ffn", "norm_final", "norm_lru_out", "norm_ssm_out",
                                                      "lru_ba", "lru_bx", "ssm_b_glu")]
                                + [cols(f["conv_w"][k]) for k in range(CONV_W)] + [cols(f["conv_b"]), cols(f["lru_lambda"])],
                                axis=1)
    wg = np.zeros((P, 2, KL, P), np.float32)
    for g, k in enumerate(("lru_wa", "lru_wx")):
        for h in range(8):
            o = 64 * (h % 2)
            wg[o:o + 64, g, h // 2, o:o + 64] = f[k][h]
    out["w_gates"] = wg

    def two(re, im):
        return np.concatenate([np.moveaxis(re, 1, 0), np.moveaxis(im, 1, 0)], axis=0)

    lr, li = f["ssm_lambda_re"], f["ssm_lambda_im"]
    out["p5"] = np.stack([two(lr, lr), two(li, li), np.broadcast_to(f["ssm_log_dt"], (P, G))], axis=1)
    br, bi = f["ssm_b_re"], f["ssm_b_im"]
    cr, ci = f["ssm_c_re"].transpose(0, 2, 1), f["ssm_c_im"].transpose(0, 2, 1)
    out["bc"] = np.stack([two(br, bi), two(bi, br), two(cr, ci), two(ci, cr)], axis=1)
    out["dsk"] = f["ssm_d"].reshape(G, HG).T
    c5 = np.zeros((P, G, 2), np.float32)
    c5[:, :, 1] = two(f["state_ssm_re"][0], f["state_ssm_im"][0])
    out["carry5"] = c5
    cs = np.zeros((P, KL, 2, CONV_W - 1), np.float32)
    cs[:, :, 1, :] = f["state_conv"][0].reshape(CONV_W - 1, KL, P).transpose(2, 1, 0)
    out["conv_st"] = cs
    ls = np.zeros((P, KL, 2), np.float32)
    ls[:, :, 1] = cols(f["state_lru"][0])
    out["lru_st"] = ls
    out["ident"] = np.eye(P, dtype=np.float32)
    out["swap"] = np.roll(np.eye(P, dtype=np.float32), NP_, axis=0)
    mask = np.ones(NW, np.float32)
    mask[[0, CS]] = 0
    out["lmask"] = np.broadcast_to(mask, (P, NW))
    out["jrow"] = np.broadcast_to(np.concatenate([np.arange(CS), np.arange(NW - CS)]).astype(np.float32), (P, NW))
    out["kf"] = np.broadcast_to(np.array([7, 6, 5, 4, 3, 2, 1, 0, *range(9)], np.float32), (P, NPOW))
    out["sgn"] = np.where(np.arange(P) < NP_, -1, 1).astype(np.float32)[:, None]
    return {k: np.ascontiguousarray(x) for k, x in out.items()}


def kernel(**inputs):
    import numpy as np
    import concourse.bacc as bacc
    from concourse.bass_utils import run_bass_kernel_spmd

    nc = bacc.Bacc("TRN2", target_bir_lowering=False, num_devices=1)
    arrays = {f"in_{k}": x for k, x in _layout(inputs).items()}
    a = {k[3:]: nc.dram_tensor(k, x.shape, F32, kind="ExternalInput").ap() for k, x in arrays.items()}
    shapes = {"y": (BLOCKS, P, KD, TB), "s5": (P, G, 2), "conv": (P, KL, 2, CONV_W - 1), "lru": (P, KL, 2)}
    outs = {k: nc.dram_tensor(f"out_{k}", s, F32, kind="ExternalOutput").ap() for k, s in shapes.items()}
    build(nc, a, outs)
    r = run_bass_kernel_spmd(nc, [arrays], core_ids=[0]).results[0]
    y, s5, conv, lru = (np.asarray(r[f"out_{k}"]) for k in ("y", "s5", "conv", "lru"))
    y = y.transpose(0, 3, 2, 1).reshape(BLOCKS, TB, D)
    y_prompt = np.ascontiguousarray(y[:, 0:TP].reshape(1, SEQ, D))
    y_sample = np.ascontiguousarray(y[:, S0:TB].reshape(1, DEC_SEQ, D))
    states = []
    for s in range(2):
        c = conv[:, :, s, :].transpose(2, 1, 0).reshape(1, 1, CONV_W - 1, LRU_W)
        h = lru[:, :, s].T.reshape(1, 1, LRU_W)
        re, im = s5[0:NP_, :, s].T[None, None], s5[NP_:P, :, s].T[None, None]
        states += [np.ascontiguousarray(x) for x in (c, h, re, im)]
    return (y_prompt, y_sample, *states)
```

```python
import math
from contextlib import ExitStack

import concourse.bass as bass
from concourse import mybir

F32 = mybir.dt.float32
F32R = mybir.dt.float32r
ALU = mybir.AluOpType
ACT = mybir.ActivationFunctionType

P = 128
D = 1024
SEQ, DEC_SEQ = 2048, 32
BLOCKS = 2
L = 8
TP, TS = SEQ // BLOCKS, DEC_SEQ // BLOCKS
PAD = L
S0 = TP + PAD
TB = S0 + TS
PIECES = [(0, 352), (352, 352), (704, TB - 704)]
NPC = len(PIECES)
NC = TB // L
CP, CS = TP // L, S0 // L
NW = NC + 1
KD = D // P
LRU_W = SSM_W = 512
KL = LRU_W // P
G, HG, NP_ = 32, 16, 64
GP = G // 2
GE = P // HG
D_FF = 2816
NF = D_FF // P
NI = NF // 2
CONV_W = 4
LRU_C = 8.0
EPS = 1e-6
ACC, AUX = 6, 2
SP5 = 5 * P + 2 * NW
NPOW = 8 + 9
LN_TERMS = 9
MAGIC = 1.5 * 2.0 ** 23
MAGIC12 = 1.5 * 2.0 ** 11
TWO_PI = 2.0 * math.pi
PI_A = 6.28125
PI_B = 0.0019350051879882812
PI_C = TWO_PI - PI_A - PI_B

IN_ORDER = [("us", 0), ("us", 1), ("us", 2), ("us", 3), ("xl", 0), ("xl", 1), ("gl", 0), ("gl", 1),
            ("xl", 2), ("xl", 3), ("gl", 2), ("gl", 3)]
PHASE1 = [("us", 0), ("us", 1), ("us", 2), ("us", 3), ("xl", 0), ("xl", 1), ("gl", 0), ("gate", 0),
          ("gl", 1), ("gate", 1), ("xl", 2), ("xl", 3), ("gl", 2), ("gate", 2), ("gl", 3), ("gate", 3)]
NSMALL = 12 + KL + KD
NCH = {"n1": KD, "nl": KL, "ns": KL, "n2": KD, "nf": KD}
NORMS = [("n1", 0)]
for _b in range(BLOCKS):
    NORMS += [("nl", _b), ("ns", _b), ("n2", _b)] + [("n1", _b + 1)] * (_b + 1 < BLOCKS) + [("nf", _b)]


def before(b, which, count):
    return sum(count(w) for w, _ in NORMS[:NORMS.index((which, b))])


def acc_order():
    order = []
    for kind, j in PHASE1:
        for p in range(NPC):
            if kind == "gate":
                order += [("r", j, p), ("ig", j, p)]
            else:
                order.append((kind, j, p))
    for t in range(GP + 2):
        if t >= 2:
            order.append(("y5", t - 2, 0))
        if t < GP:
            order += [("v1", t, 0), ("v2", t, 0)]
    order += [("glu", j, p) for j in range(KL) for p in range(NPC)]
    order += [("out", d, p) for d in range(KD) for p in range(NPC)]
    return {key: n for n, key in enumerate(order)}


ACC_AT = acc_order()
ACC_MIX = len(ACC_AT)
ACC_BLOCK = ACC_MIX + NI * 4 * NPC
AUX_AT = {key: n for n, key in enumerate(
    [("fin", 0, 0)] + [(w, 0, p) for w in ("nl", "ns", "n2") for p in range(NPC)])}
AUX_MIX = len(AUX_AT)
AUX_BLOCK = AUX_MIX + NI * KD * NPC + 2 * NPC
AUX_FFN = NPC + AUX_MIX
assert ACC_MIX % ACC == 0 and ACC_BLOCK % ACC == 0, (ACC_MIX, ACC_BLOCK)
assert AUX_BLOCK % AUX == 0 and (KD * NPC) % AUX == 0 and 4 * NPC % ACC == 0


def build(nc, a, outs):
    with ExitStack() as ctx:
        def sem(name):
            return ctx.enter_context(nc.semaphore(name))

        def at(name, shape, dt, offset):
            return nc.alloc_sbuf_tensor_at(name, shape, dt, offset=offset)

        top = [(nc.sbuf_base + 31) // 32 * 32]

        def take(nbytes):
            top[0] += (nbytes + 31) // 32 * 32
            return top[0] - (nbytes + 31) // 32 * 32

        def sb(name, shape, dt=F32):
            return at(name, shape, dt, take(4 * math.prod(shape[1:])))

        RB = TB * 4
        x_acc = sb("x_acc", [P, KD, TB])
        ones = sb("ones", [P, P])
        ident = sb("ident", [P, P])
        swap = sb("swap", [P, P])
        lmask = sb("lmask", [P, NW])
        w_gates = sb("w_gates", [P, 2, KL, P])
        vec = sb("vec", [P, 68])
        small = sb("small", [P, 20])
        carry5 = sb("carry5", [P, G, 2])
        rho = sb("rho", [P, G])
        fin5 = sb("fin5", [P, 2, G, 2])
        conv_st = sb("conv_st", [P, KL, 2, CONV_W - 1])
        lru_st = sb("lru_st", [P, KL, 2])
        B = take(2 * KD * RB)
        act_hl = at("act_hl", [P, 2, KD, TB], F32R, B)
        u5 = at("u5", [P, G, NC], F32, B)
        g5 = at("g5", [P, G, NC], F32, B + G * NC * 4)
        s5ring = at("s5ring", [P, 4, 2, SP5], F32, B + 2 * G * NC * 4)
        C = take(0)
        sw_raw = at("sw_raw", [P, 2, D], F32, C)
        sw_hl = at("sw_hl", [P, 2, 2, D], F32R, C + 8192)
        zs = at("zs", [P, KL, L, NC], F32, C + 24576)
        y_lru = at("y_lru", [P, KL, TB], F32, C + 24576 + 4 * RB)
        LT = C + 24576 + 8 * RB
        tmp = at("tmp", [P, 10, TB], F32, LT)
        xl = at("xl", [P, 3 + TB], F32, LT + 10 * RB)
        sig2 = at("sig2", [P, TB], F32, LT + 10 * RB)
        g_hl = at("g_hl", [P, 2, KL, TB], F32R, LT)
        s5tmp = at("s5tmp", [P, 2, 7, 2, NW], F32, LT)
        gu_hl = [at(f"gu_hl{i}", [P, 2, 2 * D], F32R, C + o) for i, o in enumerate((24576, 0))]
        dn_hl = [at(f"dn_hl{i}", [P, 2, D], F32R, C + o) for i, o in enumerate((40960, 16384))]
        f_tmp = at("f_tmp", [P, 6, 352], F32, C + 49152)
        rstd1 = at("rstd1", [P, TB], F32, LT + 2 * RB)
        rstd2 = at("rstd2", [P, TB], F32, LT + 10 * RB)
        f_raw = at("f_raw", [P, 2, 3 * D], F32, LT)
        ff_hl = at("ff_hl", [P, 2, 2, TB], F32R, LT + 6 * RB)
        END = LT + 10 * RB + (3 + TB) * 4
        assert C + 49152 + 6 * 352 * 4 <= LT and 6 * D * 4 <= 6 * RB and END <= nc.sbuf_usable_end, (END, nc.sbuf_usable_end)
        tb = [at(f"tb{i}", [P, G, NW], F32, B + i * G * NW * 4) for i in range(3)]
        btT = at("btT", [P, G, P], F32, B + 3 * G * NW * 4)
        pt = [at(f"pt{i}", [P, G, NPOW], F32, B + i * G * NPOW * 4) for i in range(4)]
        pz = at("pz", [P, 20, G], F32, B + 16384)
        dd = at("dd", [HG, G, HG], F32, B + 24576)
        zero = at("zero", [HG, G, 7 * HG], F32, B + 28672)
        kf = at("kf", [P, NPOW], F32, B + 43520)
        dsk = at("dsk", [HG, G], F32, B + 44544)
        SU = C + 24576
        bt = [at(f"bt{i}", [P, G, 9, HG], F32, SU + i * 18432) for i in range(2)]
        kj = at("kj", [HG, G, 8, HG], F32, SU + 2 * 18432)
        SV = SU + 2 * 18432 + 16384
        bc = at("bc", [P, 4, G, HG], F32, SV)
        bb = at("bb", [P, 4, G, HG], F32, SV + 8192)
        pw = at("pw", [P, 3, G, NPOW], F32, SV + 16384)
        jrow = at("jrow", [P, NW], F32, SV + 16384 + 3 * G * NPOW * 4)
        p5 = at("p5", [P, 3, G], F32, SV + 16384 + 3 * G * NPOW * 4 + 544)
        tau = at("tau", [P, 3, G], F32, SV + 16384 + 3 * G * NPOW * 4 + 544 + 3 * G * 4)
        assert SV + 16384 + 3 * G * NPOW * 4 + 544 + 6 * G * 4 <= nc.sbuf_usable_end

        acc = ctx.enter_context(nc.psum_tensor("acc", [P, ACC, 512], F32))
        aux = ctx.enter_context(nc.psum_tensor("aux", [P, AUX, 512], F32))
        z_dram = nc.dram_tensor("z_dram", (BLOCKS, L, HG, G, NC), F32).ap()
        g_dram = nc.dram_tensor("g_dram", (BLOCKS, L, HG, G, NC), F32).ap()
        k_dram = nc.dram_tensor("k_dram", (HG, G, 15 * HG), F32).ap()
        s5_dram = nc.dram_tensor("s5_dram", (P, G, SP5), F32).ap()

        G_MIX, G_FFN, G_FIN, G_LRU, G_SSM = 0, 8, 16, 24, 28
        B_A, B_X, B_GLU, CONV, CONVB, LAM = 32, 36, 40, 44, 60, 64
        SGN, NS2PI, HPI, CL, NCL, N2CL = 0, 1, 2, 4, 8, 12
        btmp = at("btmp", [P, 4, TB], F32, B + 4 * RB)

        def v1(c):
            return vec[:, c:c + 1]

        def sm(c):
            return small[:, c:c + 1]

        par_in = sem("par_in")
        consts = sem("consts")
        dt_done, ang_done, pow_done = sem("dt_done"), sem("ang_done"), sem("pow_done")
        s1_done, k_prod, k_done, kj_done = sem("s1_done"), sem("k_prod"), sem("k_done"), sem("kj_done")
        bt_done, bt_turned, btT_done = sem("bt_done"), sem("bt_turned"), sem("btT_done")
        s2_done, tab_done, cos_done, sin_done = sem("s2_done"), sem("tab_done"), sem("cos_done"), sem("sin_done")
        kj_st = sem("kj_st")
        s1_st = sem("s1_st")
        s5_st = sem("s5_st")
        t_st = sem("t_st")
        x_in = sem("x_in")
        sw_in = [sem(f"sw_in{i}") for i in range(2)]
        sw_hi, sw_lo = sem("sw_hi"), sem("sw_lo")
        acc_full = sem("acc_full")
        acc_free = [sem(f"acc_free{i}") for i in range(ACC)]
        aux_full = sem("aux_full")
        aux_free = [sem(f"aux_free{i}") for i in range(AUX)]
        v_step, a_step = sem("v_step"), sem("a_step")
        sq_done, sum_done = sem("sq_done"), sem("sum_done")
        xs_in = [sem(f"xs_in{i}") for i in range(2)]
        xg_hi, xg_lo = sem("xg_hi"), sem("xg_lo")
        rec_done, rstd_done = sem("rec_done"), sem("rstd_done")
        nrm, nrm_hi, nrm_lo = sem("nrm"), sem("nrm_hi"), sem("nrm_lo")
        conv_done, bx_done, gates_done, q_done, sqrt_done = sem("conv_done"), sem("bx_done"), sem("gates_done"), sem("q_done"), sem("sqrt_done")
        ylru_done = sem("ylru_done")
        z_st, u_in = [sem(f"z_st{i}") for i in range(KL)], [sem(f"u_in{i}") for i in range(KL)]
        ring_in = [sem(f"ring_in{i}") for i in range(4)]
        data0_done, w_done, p_made, p_done = sem("data0_done"), sem("w_done"), sem("p_made"), sem("p_done")
        glz_done = sem("glz_done")
        g_st, ys_in = sem("g_st"), [sem(f"ys_in{i}") for i in range(KL)]
        g_hi, g_lo, yssm_done = sem("g_hi"), sem("g_lo"), sem("yssm_done")
        fr_in = [sem(f"fr_in{i}") for i in range(2)]
        gu_hi, gu_lo, dn_hi, dn_lo = sem("gu_hi"), sem("gu_lo"), sem("dn_hi"), sem("dn_lo")
        silu_done, f_done, ff_hi, ff_lo = sem("silu_done"), sem("f_done"), sem("ff_hi"), sem("ff_lo")
        y_done, st_out = sem("y_done"), sem("st_out")
        y_st = [sem(f"y_st{k}") for k in range(KD)]

        block = ctx.enter_context(nc.Block())

        def acc_n(b, key):
            return b * ACC_BLOCK + ACC_AT[key]

        def aux_n(b, key):
            if key[0] == "n1":
                return key[2] if b == 0 else NPC + b * AUX_BLOCK - 2 * NPC + key[2]
            if key[0] == "nf":
                return NPC + (b + 1) * AUX_BLOCK - (NPC if b + 1 < BLOCKS else 2 * NPC) + key[2]
            return NPC + b * AUX_BLOCK + AUX_AT[key]

        def wait_acc(eng, b, key):
            eng.wait_ge(acc_full, acc_n(b, key) + 1)
            return acc_n(b, key) % ACC

        def wait_aux(eng, b, key):
            eng.wait_ge(aux_full, aux_n(b, key) + 1)
            return aux_n(b, key) % AUX

        def wait_evacuated(eng, b, key):
            eng.wait_ge(acc_free[acc_n(b, key) % ACC], acc_n(b, key) // ACC + 1)

        LASTP = NPC - 1

        def wait_chunk_used(eng, n):
            b, w = divmod(n, NSMALL)
            key = IN_ORDER[w] if w < 12 else ("glu", w - 12) if w < 12 + KL else ("out", w - 12 - KL)
            eng.wait_ge(acc_full, acc_n(b, (*key, LASTP)) + 1)

        def chunk_size(n):
            return KL * P if 12 <= n % NSMALL < 12 + KL else KD * P

        def ffn_acc(b, i, m):
            return i * (4 * NPC) + (b * ACC_BLOCK + ACC_MIX + m)

        def ffn_acc_uses(b, i, m):
            return i * (4 * NPC // ACC) + ((b * ACC_BLOCK + ACC_MIX) // ACC + m // ACC)

        def ffn_aux(b, i, m):
            return i * (KD * NPC) + (b * AUX_BLOCK + AUX_FFN + m)

        def ffn_aux_uses(b, i, m):
            return i * (KD * NPC // AUX) + (b * AUX_BLOCK + AUX_FFN + m) // AUX

        def chunk(b, i, q):
            return i * 2 + (b * NF + q)

        def sq_at(b, which):
            return before(b, which, lambda w: NCH[w])

        def sum_at(b, which):
            return before(b, which, lambda w: NCH[w] - 1)

        def nrm_at(b, which):
            return before(b, which, lambda w: KL if w in ("nl", "ns") else 0)

        def xg_at(b, which):
            return before(b, which, lambda w: KD if w in ("n1", "n2") else 0)

        def norm_n(b, which):
            return NORMS.index((which, b))

        params = ((p5[:], "p5"), (kf[:], "kf"), (bc[:], "bc"), (jrow[:], "jrow"), (dsk[:], "dsk"),
                  (ident[:], "ident"), (swap[:], "swap"), (lmask[:], "lmask"), (w_gates[:], "w_gates"),
                  (vec[:], "vec"), (small[:, SGN:SGN + 1], "sgn"), (carry5[:], "carry5"),
                  (conv_st[:], "conv_st"), (lru_st[:], "lru_st"))
        N_S5ST = 5

        @block.sync
        def _(sp):
            for dst, name in params:
                sp.dma_start(dst, a[name]).then_inc(par_in, 16)

            def load_small(n):
                if n >= 2:
                    sp.wait_ge(sw_lo, n - 1)
                w = n % NSMALL
                src = a["w_in"][w] if w < 12 else a["w_glu"][w - 12] if w < 12 + KL else a["w_out"][w - 12 - KL]
                sp.dma_start(sw_raw[:, n % 2, 0:chunk_size(n)], src).then_inc(sw_in[n % 2], 16)

            def stream_x(b):
                for k in range(KD):
                    if b and k == 0:
                        sp.wait_ge(gu_lo, b * NF)
                        sp.wait_ge(dn_lo, b * NF)
                    if k >= 2:
                        sp.wait_ge(xg_lo, xg_at(b, "n1") + k - 1)
                        sp.wait_ge(sq_done, sq_at(b, "n1") + k - 1)
                    sp.dma_start(tmp[:, k % 2, :], a["x"][b][:, k, :]).then_inc(xs_in[k % 2], 16)
                    if k == 1:
                        if b:
                            sp.wait_ge(acc_full, ffn_acc(b - 1, NI - 1, 4 * NPC))
                        load_small(b * NSMALL)
                        load_small(b * NSMALL + 1)

            for b in range(BLOCKS):
                if b == 0:
                    sp.wait_ge(s1_st, 16)
                    sp.wait_ge(s5_st, 16 * N_S5ST)
                stream_x(b)
                for w in range(2, 14):
                    load_small(b * NSMALL + w)
                    if b == 0 and w == 2:
                        sp.wait_ge(kj_st, 32)
                        for s in range(L):
                            sp.dma_start(s5_dram[s * HG:(s + 1) * HG, :, 4 * P:5 * P],
                                         k_dram[:, :, (7 - s) * HG:(7 - s) * HG + P]).then_inc(t_st, 16)
                wait_chunk_used(sp, b * NSMALL + 11)
                if b == 0:
                    sp.wait_ge(t_st, 16 * L)
                def heads_back(e):
                    wait_evacuated(sp, b, ("y5", 4 * e + 3, 0))
                    sp.dma_start(g_dram[b].rearrange("s h g c -> (s h) g c")[:, e * GE:(e + 1) * GE, :],
                                 g5[:, e * GE:(e + 1) * GE, :]).then_inc(g_st, 16)
                    sp.wait_ge(g_st, 16 * (b * KL + e + 1))
                    sp.wait_ge(z_st[e], 16 * GE * (b + 1))
                    for gl in range(GE):
                        sp.dma_start(zs[gl * HG:(gl + 1) * HG, e, :, :],
                                     g_dram[b][:, :, e * GE + gl, :].rearrange("s h c -> h s c"))\
                          .then_inc(ys_in[e], 16)

                for t in range(GP):
                    if t >= 8 and t % 4 == 0:
                        heads_back(t // 4 - 2)
                    if t % 4 == 0:
                        sp.wait_ge(z_st[t // 4], 16 * GE * (b + 1))
                        sp.dma_start(u5[:, 2 * t:2 * t + 8, :],
                                     z_dram[b].rearrange("s h g c -> (s h) g c")[:, 2 * t:2 * t + 8, :])\
                          .then_inc(u_in[t // 4], 16)
                    if t >= 4:
                        wait_acc(sp, b, ("y5", t - 4, 0))
                    sp.dma_start(s5ring[:, t % 4, :, :], s5_dram[:, 2 * t:2 * t + 2, :]).then_inc(ring_in[t % 4], 16)
                heads_back(2)
                heads_back(3)
                if b:
                    for k in range(KD):
                        sp.wait_ge(y_st[k], 16 * b)
                sp.dma_start(x_acc[:], a["x"][b]).then_inc(x_in, 16)
                for w in range(14, NSMALL):
                    load_small(b * NSMALL + w)
                    if w == 12 + KL + 1:
                        wait_acc(sp, b, ("glu", KL - 1, LASTP))
                        for q in range(2):
                            sp.dma_start(f_raw[:, q, :], a["w_ffn"][q]).then_inc(fr_in[q], 16)
                with sp.Fori(0, NI - 1) as i:
                    for q in range(2):
                        sp.wait_ge(gu_lo, chunk(b, i, q) + 1)
                        sp.wait_ge(dn_lo, chunk(b, i, q) + 1)
                        src = a["w_ffn"][bass.ds(i * 2 + (2 + q), 1)].rearrange("a p n -> (a p) n")
                        sp.dma_start(f_raw[:, q, :], src).then_inc(fr_in[q], 16)

        @block.gpsimd
        def _(po):
            po.memset(ones[:], 1.0).then_inc(consts, 1)
            po.memset(small[:, HPI:HPI + 1], math.pi / 2).then_inc(consts, 1)
            po.memset(zero[:], 0.0).then_inc(consts, 1)
            po.wait_ge(consts, 3)
            po.dma_start(k_dram[:, :, 0:7 * HG], zero[:]).then_inc(kj_st, 16)
            po.wait_ge(s1_done, 1)
            po.dma_start(s5_dram[:, :, 2 * P:3 * P], bt[1][:, :, 1:9, :].rearrange("p g t h -> p g (t h)"))\
              .then_inc(s1_st, 16)
            po.wait_ge(kj_done, 1)
            po.dma_start(k_dram[:, :, 7 * HG:15 * HG], kj[:].rearrange("h g j c -> h g (j c)")).then_inc(kj_st, 16)
            po.wait_ge(btT_done, 8)
            po.dma_start(s5_dram[:, :, 0:P], btT[:]).then_inc(s5_st, 16)
            po.wait_ge(btT_done, 16)
            po.dma_start(s5_dram[:, :, P:2 * P], btT[:]).then_inc(s5_st, 16)
            po.wait_ge(s2_done, 1)
            po.dma_start(s5_dram[:, :, 3 * P:4 * P], bt[1][:, :, 1:9, :].rearrange("p g t h -> p g (t h)"))\
              .then_inc(s5_st, 16)
            po.wait_ge(cos_done, 1)
            po.dma_start(s5_dram[:, :, 5 * P:5 * P + NW], tb[1][:]).then_inc(s5_st, 16)
            po.wait_ge(sin_done, 1)
            po.dma_start(s5_dram[:, :, 5 * P + NW:SP5], tb[2][:]).then_inc(s5_st, 16)

            def store_y(b, ks):
                for k in ks:
                    po.wait_ge(y_done, b * KD + k + 1)
                    po.dma_start(outs["y"][b][:, k, :], x_acc[:, k, :]).then_inc(y_st[k], 16)

            for b in range(BLOCKS):
                for e in range(KL):
                    for p in range(NPC):
                        wait_evacuated(po, b, ("us", e, p))
                    for gl in range(GE):
                        po.dma_start(z_dram[b][:, :, e * GE + gl, :].rearrange("s h c -> h s c"),
                                     zs[gl * HG:(gl + 1) * HG, e, :, :]).then_inc(z_st[e], 16)
                    if b and e in (1, 2):
                        store_y(b - 1, range(4 * e - 4, 4 * e))
                for t in range(GP):
                    s, tab = s5tmp[:, t % 2], s5ring[:, t % 4]
                    po.wait_ge(w_done, b * GP + t + 1)
                    if t >= 2:
                        wait_acc(po, b, ("y5", t - 2, 0))
                    po.tensor_tensor(s[:, 4], s[:, 3], tab[:, :, 5 * P:5 * P + NW], ALU.mult)
                    po.tensor_tensor(s[:, 5], s[:, 3], tab[:, :, 5 * P + NW:SP5], ALU.mult).then_inc(p_made, 1)
                    po.wait_ge(p_made, b * GP + t + 1)
                    po.tensor_copy(fin5[:, 0, 2 * t:2 * t + 2, :], s[:, 4, :, CP:NW:NW - 1 - CP])
                    po.tensor_copy(fin5[:, 1, 2 * t:2 * t + 2, :], s[:, 5, :, CP:NW:NW - 1 - CP]).then_inc(p_done, 1)
                def hidden(b, i):
                    for q in range(2):
                        for p, (t0, n) in enumerate(PIECES):
                            po.wait_ge(silu_done, i * (2 * NPC) + (b * NI * 2 * NPC + q * NPC + p + 1))
                            m = q * 2 * NPC + 2 * p + 1
                            po.wait_ge(acc_free[m % ACC], ffn_acc_uses(b, i, m) + 1)
                            po.tensor_tensor(f_tmp[:, 3 + p, 0:n], f_tmp[:, p, 0:n], f_tmp[:, 3 + p, 0:n], ALU.mult)\
                              .then_inc(f_done, 1)

                with po.Fori(0, NI) as i:
                    hidden(b, i)
            store_y(BLOCKS - 1, range(KD))
            po.dma_start(outs["s5"], carry5[:]).then_inc(st_out, 16)
            po.dma_start(outs["conv"], conv_st[:]).then_inc(st_out, 16)
            po.dma_start(outs["lru"], lru_st[:]).then_inc(st_out, 16)
            po.wait_ge(st_out, 48)
            for k in range(KD):
                po.wait_ge(y_st[k], 16 * BLOCKS)

        @block.scalar
        def _(act):
            steps = [0]

            def link(ins):
                steps[0] += 1
                ins.then_inc(a_step, 1)
                act.wait_ge(a_step, steps[0])

            act.wait_ge(par_in, 16 * len(params))
            act.wait_ge(consts, 3)
            link(act.activation(pz[:, 16, 0:KL], vec[:, LAM:LAM + KL], ACT.Abs))
            act.activation(pz[:, 17, 0:KL], pz[:, 16, 0:KL], ACT.Exp, scale=-1.0)
            act.activation(pz[:, 0, :], p5[:, 2, :], ACT.Exp).then_inc(dt_done, 1)
            act.wait_ge(ang_done, 1)
            act.activation(rho[:], pz[:, 1, :], ACT.Exp, scale=float(L))
            link(act.activation(pt[2][:], pt[1][:], ACT.Exp))
            act.activation(pt[3][:], pt[0][:], ACT.Sin)
            link(act.activation(pt[1][:], pt[0][:], ACT.Abs))
            act.activation(pt[0][:], pt[1][:], ACT.Sin, bias=sm(HPI), scale=-1.0).then_inc(pow_done, 1)
            for n in range(16):
                act.wait_ge(bt_turned, n + 1)
                if n == 8:
                    act.wait_ge(s5_st, 16)
                act.activation(btT[:, 4 * (n % 8):4 * (n % 8) + 4, :].rearrange("p g c -> p (g c)"),
                               acc[:, (8 + n) % ACC, :], ACT.Copy).then_inc(btT_done, 1)
            act.wait_ge(tab_done, 1)
            link(act.activation(tb[2][:], tb[0][:], ACT.Abs))
            act.activation(tb[1][:], tb[2][:], ACT.Sin, bias=sm(HPI), scale=-TWO_PI).then_inc(cos_done, 1)
            act.wait_ge(cos_done, 1)
            act.activation(tb[2][:], tb[0][:], ACT.Sin, scale=sm(NS2PI)).then_inc(sin_done, 1)

            def small_hi(n):
                act.wait_ge(sw_in[n % 2], 16 * (n // 2 + 1))
                if n >= 2:
                    wait_chunk_used(act, n - 2)
                act.activation(sw_hl[:, n % 2, 0, 0:chunk_size(n)], sw_raw[:, n % 2, 0:chunk_size(n)],
                               ACT.Copy).then_inc(sw_hi, 1)

            def square(b, which, k, src, slots):
                if k >= 2:
                    act.wait_ge(sum_done, sum_at(b, which) + max(1, k - 2))
                act.activation(slots[k % 2], src, ACT.Square).then_inc(sq_done, 1)

            def rsqrt(b, which, dst):
                act.wait_ge(rec_done, norm_n(b, which) + 1)
                act.activation(dst, dst, ACT.Sqrt).then_inc(rstd_done, 1)

            def gain_hi(b, which, k, gain, src):
                act.activation(act_hl[:, 0, k, :], src, ACT.Copy, scale=v1(gain + k)).then_inc(xg_hi, 1)

            def stream_x(b, k):
                act.wait_ge(xs_in[k % 2], 16 * (b * KD // 2 + k // 2 + 1))
                if b and k == 0:
                    act.wait_ge(acc_full, ffn_acc(b - 1, NI - 1, 4 * NPC))
                gain_hi(b, "n1", k, G_MIX, tmp[:, k % 2, :])
                square(b, "n1", k, tmp[:, k % 2, :], [tmp[:, 3, :], tmp[:, 4, :]])

            def norm_hi(b, which, k, src, dst):
                act.wait_ge(nrm, nrm_at(b, which) + k + 1)
                act.activation(dst, src, ACT.Copy).then_inc(nrm_hi, 1)

            def pair_curves(b, j0):
                for j in (j0, j0 + 1):
                    act.wait_ge(bx_done, b * KL + j + 1)
                    act.activation(tmp[:, 6 + j % 2, :], tmp[:, 8 + j % 2, :], ACT.Tanh, scale=sm(CL + j))
                for j in (j0, j0 + 1):
                    act.activation(tmp[:, 4 + j % 2, :], tmp[:, 8 + j % 2, :], ACT.Exp, scale=sm(NCL + j))
                    act.activation(tmp[:, 8 + j % 2, :], tmp[:, 8 + j % 2, :], ACT.Exp, scale=sm(N2CL + j))\
                       .then_inc(gates_done, 1)

            def pair_sqrt(b, j0):
                for j in (j0, j0 + 1):
                    act.wait_ge(q_done, b * KL + j + 1)
                    act.activation(tmp[:, 6 + j % 2, :], tmp[:, 6 + j % 2, :], ACT.Sqrt).then_inc(sqrt_done, 1)

            def gu_split(b, i, q):
                act.wait_ge(fr_in[q], i * 16 + 16 * (b * NI + 1))
                act.activation(gu_hl[q][:, 0, :], f_raw[:, q, 0:2 * D], ACT.Copy).then_inc(gu_hi, 1)

            def ffn(b, i, last):
                act.wait_ge(aux_full, ffn_aux(b, i, 0))
                for q in range(2):
                    act.activation(dn_hl[q][:, 0, :], f_raw[:, q, 2 * D:3 * D], ACT.Copy).then_inc(dn_hi, 1)
                for q in range(2):
                    def hidden_hi(p):
                        t0, n = PIECES[p]
                        act.wait_ge(f_done, i * (2 * NPC) + (b * NI * 2 * NPC + q * NPC + p + 1))
                        act.activation(ff_hl[:, q, 0, t0:t0 + n], f_tmp[:, 3 + p, 0:n], ACT.Copy).then_inc(ff_hi, 1)

                    for p, (t0, n) in enumerate(PIECES):
                        m = q * 2 * NPC + 2 * p
                        act.wait_ge(acc_free[m % ACC], ffn_acc_uses(b, i, m) + 1)
                        act.activation(f_tmp[:, p, 0:n], f_tmp[:, p, 0:n], ACT.Silu).then_inc(silu_done, 1)
                        if p:
                            hidden_hi(p - 1)
                    hidden_hi(NPC - 1)
                    if not last:
                        act.wait_ge(acc_full, ffn_acc(b, i, (q + 1) * 2 * NPC))
                        gu_split(b, i + 1, q)

            def final_squares(b):
                for m in range(KD * NPC - 2, KD * NPC):
                    bank = (b * AUX_BLOCK + AUX_FFN + m) % AUX
                    act.wait_ge(aux_free[bank], ffn_aux_uses(b, NI - 1, m) + 1)
                for k in range(KD):
                    square(b, "nf", k, x_acc[:, k, :], [tmp[:, 8, :], tmp[:, 9, :]])

            def natural(ap):
                return ap.rearrange("p s c -> p c s")

            def tokens(ap):
                return ap.rearrange("p (c s) -> p c s", s=L)

            for b in range(BLOCKS):
                w0 = b * NSMALL
                if b == 0:
                    for k in range(KD):
                        if k == 2:
                            small_hi(w0)
                        stream_x(b, k)
                    small_hi(w0 + 1)
                if b:
                    final_squares(b - 1)
                rsqrt(b, "n1", rstd1[:])
                for kind, j in PHASE1:
                    if kind == "gate":
                        for p, (t0, n) in enumerate(PIECES):
                            for g, slot, bias in (("r", 8, B_A), ("ig", 0, B_X)):
                                bank = wait_acc(act, b, (g, j, p))
                                if j >= 2:
                                    act.wait_ge(ylru_done, b * KL + j - 1)
                                act.activation(tmp[:, slot + j % 2, t0:t0 + n], acc[:, bank, 0:n], ACT.Sigmoid,
                                               bias=v1(bias + j)).then_inc(acc_free[bank], 1)
                        if j % 2:
                            pair_curves(b, j - 1)
                        if j == 3:
                            pair_sqrt(b, 2)
                        continue
                    for p, (t0, n) in enumerate(PIECES):
                        if kind == "gl":
                            wait_evacuated(act, b, (kind, j, p))
                            act.activation(y_lru[:, j, t0:t0 + n], y_lru[:, j, t0:t0 + n], ACT.Gelu_apprx_tanh)\
                               .then_inc(glz_done, 1)
                    w = IN_ORDER.index((kind, j))
                    small_hi(w0 + w + 2)
                    if b and w == 0:
                        rsqrt(b - 1, "nf", tmp[:, 7, :])
                    if (kind, j) == ("xl", 2):
                        pair_sqrt(b, 0)
                for t in range(GP + 2):
                    if t < GP:
                        if t == 0:
                            act.wait_ge(ylru_done, KL * (b + 1))
                        if t >= 2:
                            act.wait_ge(w_done, b * GP + t - 1)
                        for q in range(2):
                            act.activation(s5tmp[:, t % 2, 6, q, :], lmask[:], ACT.Copy,
                                           scale=rho[:, 2 * t + q:2 * t + q + 1]).then_inc(data0_done, 1)
                    if t < 2:
                        continue
                    t -= 2
                    bank = wait_acc(act, b, ("y5", t, 0))
                    act.activation(g5[:, 2 * t:2 * t + 2, :].rearrange("p q c -> p (q c)"), acc[:, bank, 0:2 * NC],
                                   ACT.Gelu_apprx_tanh).then_inc(acc_free[bank], 1)
                for j in range(KL):
                    square(b, "nl", j, y_lru[:, j, :], [tmp[:, 9, :], sig2[:]])
                for j in range(KL):
                    act.wait_ge(ys_in[j], 16 * GE * (b + 1))
                    act.activation(tokens(g_hl[:, 0, j, :]), natural(zs[:, j, :, :]), ACT.Copy).then_inc(g_hi, 1)
                rsqrt(b, "nl", tmp[:, 8, :])
                for j in range(KL):
                    norm_hi(b, "nl", j, y_lru[:, j, :], act_hl[:, 0, j, :])
                for j in range(KL):
                    sig = btmp[:, 3, :] if j % 2 == 0 else sig2[:]
                    for p, (t0, n) in enumerate(PIECES):
                        bank = wait_acc(act, b, ("glu", j, p))
                        if j >= 2:
                            act.wait_ge(yssm_done, b * KL + j - 1)
                        act.activation(sig.rearrange("p (s c) -> p s c", s=L)[:, :, t0 // L:(t0 + n) // L],
                                       acc[:, bank, 0:n].rearrange("p (c s) -> p s c", s=L), ACT.Sigmoid,
                                       bias=v1(B_GLU + j)).then_inc(acc_free[bank], 1)
                    small_hi(w0 + 12 + j + 2)
                    act.wait_ge(yssm_done, b * KL + j + 1)
                    square(b, "ns", j, zs[:, j, :, :].rearrange("p s c -> p (s c)"), [btmp[:, 0, :], btmp[:, 1, :]])
                rsqrt(b, "ns", tmp[:, 9, :])
                for j in range(KL):
                    norm_hi(b, "ns", j, natural(zs[:, j, :, :]), tokens(act_hl[:, 0, KL + j, :]))
                for d in range(KD):
                    wait_evacuated(act, b, ("out", d, LASTP))
                    if d < KD - 1:
                        square(b, "n2", d, x_acc[:, d, :], [tmp[:, 8, :], tmp[:, 9, :]])
                    if d + 2 < KD:
                        small_hi(w0 + 12 + KL + d + 2)
                    if d == 3:
                        gu_split(b, 0, 0)
                for k in range(KD):
                    gain_hi(b, "n2", k, G_FFN, x_acc[:, k, :])
                    if k == 0:
                        square(b, "n2", KD - 1, x_acc[:, KD - 1, :], [tmp[:, 8, :], tmp[:, 9, :]])
                gu_split(b, 0, 1)
                rsqrt(b, "n2", rstd2[:])
                with act.Fori(0, NI - 1) as i:
                    ffn(b, i, False)
                ffn(b, NI - 1, True)
                if b + 1 < BLOCKS:
                    for k in range(KD):
                        if k == 2:
                            small_hi(w0 + NSMALL)
                        stream_x(b + 1, k)
                    act.wait_ge(aux_full, ffn_aux(b, NI - 1, KD * NPC))
                    small_hi(w0 + NSMALL + 1)
                else:
                    final_squares(b)
                    rsqrt(b, "nf", tmp[:, 7, :])

        @block.tensor
        def _(pe):
            pe.wait_ge(s1_done, 1)
            for c in range(8):
                if c >= ACC:
                    pe.wait_ge(k_done, c - ACC + 1)
                for g in range(4 * c, 4 * c + 4):
                    ins = pe.matmul(acc[0:HG, c % ACC, (g % 4) * P:(g % 4 + 1) * P], bb[:, 0, g, :],
                                    bt[1][:, g, 0:8, :].rearrange("p t h -> p (t h)"), start=True, stop=True)
                ins.then_inc(k_prod, 1)
            for n in range(16):
                pe.wait_ge(bt_done, n // 8 + 1)
                if 8 + n - ACC < 8:
                    pe.wait_ge(k_done, 8 + n - ACC + 1)
                else:
                    pe.wait_ge(btT_done, n - ACC + 1)
                for g in range(4 * (n % 8), 4 * (n % 8) + 4):
                    ins = pe.transpose(acc[:, (8 + n) % ACC, (g % 4) * P:(g % 4 + 1) * P],
                                       bt[0][:, g, 0:8, :].rearrange("p t h -> p (t h)"), ident[:])
                ins.then_inc(bt_turned, 1)
            pe.wait_ge(btT_done, 16)

            def three(out, w_hl, x_hl, first, last):
                pe.matmul(out, w_hl(0), x_hl(0), start=first, stop=False)
                pe.matmul(out, w_hl(0), x_hl(1), start=False, stop=False)
                return pe.matmul(out, w_hl(1), x_hl(0), start=False, stop=last)

            def acc_bank(b, key):
                bank, uses = acc_n(b, key) % ACC, acc_n(b, key) // ACC
                if uses:
                    pe.wait_ge(acc_free[bank], uses)
                return bank

            def aux_bank(b, key):
                bank, uses = aux_n(b, key) % AUX, aux_n(b, key) // AUX
                if uses:
                    pe.wait_ge(aux_free[bank], uses)
                return bank

            def sum_rows(b, which, src):
                for p, (t0, n) in enumerate(PIECES):
                    bank = aux_bank(b, (which, 0, p))
                    pe.matmul(aux[:, bank, 0:n], ones[:], src[:, t0:t0 + n], start=True, stop=True).then_inc(aux_full, 1)

            def small_product(b, w, key, kn, x_hl, ready=None):
                n = b * NSMALL + w
                pe.wait_ge(sw_lo, n + 1)
                for p, (t0, m) in enumerate(PIECES):
                    if w == 0 and p == LASTP:
                        pe.wait_ge(sum_done, sum_at(b, "n1") + KD - 1)
                        sum_rows(b, "n1", tmp[:, 5, :])
                    bank = acc_bank(b, (*key, p))
                    for k in range(kn):
                        if ready and p == 0:
                            ready(k)
                        ins = three(acc[:, bank, 0:m], lambda s: sw_hl[:, n % 2, s, k * P:(k + 1) * P],
                                    lambda s: x_hl[:, s, k, t0:t0 + m], k == 0, k == kn - 1)
                    ins.then_inc(acc_full, 1)

            def ffn(b, i):
                for q in range(2):
                    pe.wait_ge(gu_lo, chunk(b, i, q) + 1)
                    for p, (t0, n) in enumerate(PIECES):
                        for u in range(2):
                            m = q * 2 * NPC + 2 * p + u
                            pe.wait_ge(acc_free[m % ACC], ffn_acc_uses(b, i, m))
                            for k in range(KD):
                                c = (u * KD + k) * P
                                ins = three(acc[:, m % ACC, 0:n], lambda s: gu_hl[q][:, s, c:c + P],
                                            lambda s: act_hl[:, s, k, t0:t0 + n], k == 0, k == KD - 1)
                            ins.then_inc(acc_full, 1)
                pe.wait_ge(dn_lo, chunk(b, i, 1) + 1)
                for p, (t0, n) in enumerate(PIECES):
                    pe.wait_ge(ff_lo, i * (2 * NPC) + (b * NI * 2 * NPC + NPC + p + 1))
                    for d in range(KD):
                        m = p * KD + d
                        bank = (b * AUX_BLOCK + AUX_FFN + m) % AUX
                        pe.wait_ge(aux_free[bank], ffn_aux_uses(b, i, m))
                        for q in range(2):
                            ins = three(aux[:, bank, 0:n], lambda s: dn_hl[q][:, s, d * P:(d + 1) * P],
                                        lambda s: ff_hl[:, q, s, t0:t0 + n], q == 0, q == 1)
                        ins.then_inc(aux_full, 1)

            def final_sum(b):
                pe.wait_ge(sum_done, sum_at(b, "nf") + KD - 1)
                sum_rows(b, "nf", tmp[:, 6, :])

            for b in range(BLOCKS):
                for kind, j in PHASE1:
                    if (kind, j) == ("us", 2) and b:
                        final_sum(b - 1)
                    if kind == "gate":
                        pe.wait_ge(conv_done, b * KL + j + 1)
                        for p, (t0, n) in enumerate(PIECES):
                            for g, name in enumerate(("r", "ig")):
                                bank = acc_bank(b, (name, j, p))
                                pe.matmul(acc[:, bank, 0:n], w_gates[:, g, j, :], tmp[:, 6 + j % 2, t0:t0 + n],
                                          start=True, stop=True).then_inc(acc_full, 1)
                    else:
                        w = IN_ORDER.index((kind, j))
                        small_product(b, w, (kind, j), KD, act_hl,
                                      (lambda k: pe.wait_ge(xg_lo, xg_at(b, "n1") + k + 1)) if w == 0 else None)
                for t in range(GP + 2):
                    if t >= 2:
                        o = t - 2
                        pe.wait_ge(p_done, b * GP + o + 1)
                        bank = acc_bank(b, ("y5", o, 0))
                        for q in range(2):
                            g, out = 2 * o + q, acc[:, bank, q * NC:(q + 1) * NC]
                            par = s5ring[:, o % 4, q, :]
                            pe.matmul(out, par[:, 4 * P:5 * P], u5[:, g, :], start=True, stop=False)
                            pe.matmul(out, par[:, 2 * P:3 * P], s5tmp[:, o % 2, 4, q, 0:NC], start=False, stop=False)
                            ins = pe.matmul(out, par[:, 3 * P:4 * P], s5tmp[:, o % 2, 5, q, 0:NC], start=False, stop=True)
                        ins.then_inc(acc_full, 1)
                    if t < GP:
                        pe.wait_ge(u_in[t // 4], 16 * (b + 1))
                        pe.wait_ge(ring_in[t % 4], 16 * (b * 4 + t // 4 + 1))
                        for v in range(2):
                            bank = acc_bank(b, (("v1", "v2")[v], t, 0))
                            for q in range(2):
                                ins = pe.matmul(acc[:, bank, q * NC:(q + 1) * NC], s5ring[:, t % 4, q, v * P:(v + 1) * P],
                                                u5[:, 2 * t + q, :], start=True, stop=True)
                            ins.then_inc(acc_full, 1)
                bank = aux_bank(b, ("fin", 0, 0))
                pe.matmul(aux[:, bank, 0:2 * G], ident[:], fin5[:, 0].rearrange("p g s -> p (g s)"), start=True, stop=False)
                pe.matmul(aux[:, bank, 0:2 * G], swap[:], fin5[:, 1].rearrange("p g s -> p (g s)"), start=False,
                          stop=True).then_inc(aux_full, 1)
                pe.wait_ge(sum_done, sum_at(b, "nl") + KL - 1)
                sum_rows(b, "nl", tmp[:, 8, :])
                for j in range(KL):
                    small_product(b, 12 + j, ("glu", j), KL, g_hl,
                                  (lambda k: pe.wait_ge(g_lo, b * KL + k + 1)) if j == 0 else None)
                for half in range(2):
                    for d in range(2):
                        n = b * NSMALL + 12 + KL + d
                        pe.wait_ge(sw_lo, n + 1)
                        for p, (t0, m) in enumerate(PIECES):
                            bank = acc_bank(b, ("out", d, p)) if half == 0 else acc_n(b, ("out", d, p)) % ACC
                            for k in range(half * KL, half * KL + KL):
                                if d == 0 and p == 0:
                                    pe.wait_ge(nrm_lo, nrm_at(b, "nl") + k + 1)
                                ins = three(acc[:, bank, 0:m], lambda s: sw_hl[:, n % 2, s, k * P:(k + 1) * P],
                                            lambda s: act_hl[:, s, k, t0:t0 + m], k == 0, k == KD - 1)
                            if half:
                                ins.then_inc(acc_full, 1)
                    if half == 0:
                        pe.wait_ge(sum_done, sum_at(b, "ns") + KL - 1)
                        sum_rows(b, "ns", btmp[:, 2, :])
                for d in range(2, KD):
                    small_product(b, 12 + KL + d, ("out", d), KD, act_hl)
                pe.wait_ge(sum_done, sum_at(b, "n2") + KD - 1)
                sum_rows(b, "n2", tmp[:, 6, :])
                pe.wait_ge(xg_lo, xg_at(b, "n2") + KD)
                with pe.Fori(0, NI - 1) as i:
                    ffn(b, i)
                ffn(b, NI - 1)
            final_sum(BLOCKS - 1)

        @block.vector
        def _(v):
            steps = [0]

            def link(ins):
                steps[0] += 1
                ins.then_inc(v_step, 1)
                v.wait_ge(v_step, steps[0])

            def tt(out, x, y, op):
                return v.tensor_tensor(out, x, y, op)

            def stt(out, x, s, y, op0, op1):
                return v.scalar_tensor_tensor(out=out, in0=x, scalar=s, in1=y, op0=op0, op1=op1)

            MUL, ADD, SUB = ALU.mult, ALU.add, ALU.subtract

            def turn_down(x, n):
                link(v.tensor_scalar(n, x, 1.0 / TWO_PI, MAGIC, MUL, ADD))
                link(v.tensor_scalar(n, n, MAGIC, None, SUB))
                for part in (PI_A, PI_B, PI_C):
                    link(stt(x, n, -part, x, MUL, ADD))
                link(v.tensor_scalar(x, x, 3.1415925, -3.1415925, ALU.min, ALU.max))

            def z(n):
                return pz[:, n, :]

            v.wait_ge(dt_done, 1)
            link(tt(z(1), p5[:, 0, :], z(0), MUL))
            link(tt(z(4), p5[:, 1, :], z(0), MUL))
            turn_down(z(4), z(3))
            link(tt(pt[0][:], z(4).unsqueeze(2).broadcast_to([P, G, NPOW]),
                    kf[:].unsqueeze(1).broadcast_to([P, G, NPOW]), MUL))
            turn_down(pt[0][:], pt[2][:])
            tt(pt[1][:], z(1).unsqueeze(2).broadcast_to([P, G, NPOW]),
               kf[:].unsqueeze(1).broadcast_to([P, G, NPOW]), MUL).then_inc(ang_done, 1)
            e, t2, w2, po_ = (pz[:, n, 0:KL] for n in (17, 18, 19, 16))
            lam = vec[:, LAM:LAM + KL]
            link(v.tensor_scalar(t2, e, 2.0, None, ADD))
            link(v.reciprocal(w2, t2))
            link(tt(e, e, w2, MUL))
            link(tt(w2, e, e, MUL))
            link(v.tensor_scalar(po_, w2, 1.0 / (2 * LN_TERMS - 1), 1.0 / (2 * LN_TERMS - 3), MUL, ADD))
            for m in range(LN_TERMS - 3, -1, -1):
                link(tt(po_, po_, w2, MUL))
                link(v.tensor_scalar(po_, po_, 1.0 / (2 * m + 1), None, ADD))
            link(tt(po_, po_, e, MUL))
            link(v.tensor_scalar(t2, lam, -1.0, 0.0, MUL, ALU.max))
            link(stt(t2, po_, 2.0, t2, MUL, ADD))
            v.tensor_scalar(small[:, CL:CL + KL], t2, LRU_C, None, MUL)
            v.tensor_scalar(small[:, NCL:NCL + KL], t2, -LRU_C, None, MUL)
            v.tensor_scalar(small[:, N2CL:N2CL + KL], t2, -2.0 * LRU_C, None, MUL)
            link(v.tensor_scalar(sm(NS2PI), sm(SGN), -TWO_PI, None, MUL))
            link(v.tensor_scalar(tau[:, 0, :], z(4), L / TWO_PI, None, MUL))
            link(v.tensor_scalar(z(3), tau[:, 0, :], MAGIC, None, ADD))
            link(v.tensor_scalar(z(3), z(3), MAGIC, None, SUB))
            link(tt(tau[:, 0, :], tau[:, 0, :], z(3), SUB))
            link(v.tensor_scalar(z(3), tau[:, 0, :], MAGIC12, None, ADD))
            link(v.tensor_scalar(tau[:, 1, :], z(3), MAGIC12, None, SUB))
            link(tt(tau[:, 2, :], tau[:, 0, :], tau[:, 1, :], SUB))
            v.wait_ge(pow_done, 1)
            tt(pw[:, 0], pt[2][:], pt[0][:], MUL)
            link(tt(pw[:, 1], pt[2][:], pt[3][:], MUL))
            link(v.tensor_scalar(pw[:, 2], pw[:, 1], sm(SGN), None, MUL))
            lr, li = p5[:, 0, :], p5[:, 1, :]
            ni = z(6)
            v.tensor_copy(ni, pw[:, 1, :, 9])
            v.tensor_scalar(z(5), pw[:, 0, :, 9], 1.0, None, SUB)
            tt(z(7), lr, lr, MUL)
            link(tt(z(8), li, li, MUL))
            link(tt(z(7), z(7), z(8), ADD))
            link(v.reciprocal(z(7), z(7)))
            tt(z(8), z(5), lr, MUL)
            link(tt(z(9), ni, li, MUL))
            link(tt(z(8), z(8), z(9), ADD))
            link(tt(z(8), z(8), z(7), MUL))
            tt(z(9), ni, lr, MUL)
            link(tt(z(10), z(5), li, MUL))
            link(tt(z(9), z(9), z(10), SUB))
            link(tt(z(9), z(9), z(7), MUL))
            link(v.tensor_scalar(z(9), z(9), sm(SGN), None, MUL))

            def gh(x):
                return x.unsqueeze(2).broadcast_to([P, G, HG])

            tt(bb[:, 0], bc[:, 0], gh(z(8)), MUL)
            link(tt(bb[:, 2], bc[:, 1], gh(z(9)), MUL))
            tt(bb[:, 1], bc[:, 1], gh(z(8)), MUL)
            link(tt(bb[:, 3], bc[:, 0], gh(z(9)), MUL))
            link(tt(bb[:, 0], bb[:, 0], bb[:, 2], ADD))
            link(tt(bb[:, 1], bb[:, 1], bb[:, 3], SUB))
            link(v.tensor_scalar(bb[:, 2], bc[:, 2], sm(SGN), -1.0, MUL, MUL))
            link(v.tensor_scalar(bb[:, 3], bc[:, 3], sm(SGN), None, MUL))

            def powers(x, r, k0, kn):
                return (x.unsqueeze(2).broadcast_to([P, G, kn, HG]),
                        pw[:, r, :, k0:k0 + kn].unsqueeze(3).broadcast_to([P, G, kn, HG]))

            tt(bt[1][:], *powers(bb[:, 2], 0, 8, 9), MUL)
            link(tt(bt[0][:], *powers(bc[:, 3], 1, 8, 9), MUL))
            tt(bt[1][:], bt[1][:], bt[0][:], SUB).then_inc(s1_done, 1)
            tt(dd[:], ident[0:HG, 0:HG].unsqueeze(1).broadcast_to([HG, G, HG]),
               dsk[:].unsqueeze(2).broadcast_to([HG, G, HG]), MUL)
            for c in range(8):
                v.wait_ge(k_prod, c + 1)
                v.tensor_copy(kj[:, 4 * c:4 * c + 4].rearrange("p g j h -> p (g j h)"), acc[0:HG, c % ACC, :])\
                 .then_inc(k_done, 1)
            v.wait_ge(k_done, 8)
            tt(kj[:, :, 0, :], kj[:, :, 0, :], dd[:], ADD).then_inc(kj_done, 1)
            v.wait_ge(s1_st, 16)
            for m, (x, y, op) in enumerate(((0, 1, ADD), (1, 0, SUB))):
                if m:
                    v.wait_ge(bt_turned, 8)
                tt(bt[0][:, :, 0:8], *powers(bb[:, x], 0, 0, 8), MUL)
                link(tt(bt[1][:, :, 0:8], *powers(bb[:, y], 2, 0, 8), MUL))
                tt(bt[0][:, :, 0:8], bt[0][:, :, 0:8], bt[1][:, :, 0:8], op).then_inc(bt_done, 1)
            v.wait_ge(bt_turned, 16)
            tt(bt[1][:, :, 1:9], *powers(bb[:, 3], 0, 9, 8), MUL)
            link(tt(bt[0][:, :, 1:9], *powers(bc[:, 2], 1, 9, 8), MUL))
            tt(bt[1][:, :, 1:9], bt[1][:, :, 1:9], bt[0][:, :, 1:9], SUB).then_inc(s2_done, 1)
            jb = jrow[:].unsqueeze(1).broadcast_to([P, G, NW])
            v.wait_ge(kj_st, 32)
            tt(tb[0][:], jb, tau[:, 1, :].unsqueeze(2).broadcast_to([P, G, NW]), MUL)
            link(tt(tb[1][:], jb, tau[:, 2, :].unsqueeze(2).broadcast_to([P, G, NW]), MUL))
            link(tt(tb[2][:], tb[0][:], tb[1][:], ADD))
            link(v.tensor_scalar(tb[2][:], tb[2][:], MAGIC, None, ADD))
            link(v.tensor_scalar(tb[2][:], tb[2][:], MAGIC, None, SUB))
            link(tt(tb[0][:], tb[0][:], tb[2][:], SUB))
            link(tt(tb[0][:], tb[0][:], tb[1][:], ADD))
            v.tensor_scalar(tb[0][:], tb[0][:], 0.49999997, -0.49999997, ALU.min, ALU.max).then_inc(tab_done, 1)

            def small_lo(n):
                v.wait_ge(sw_hi, n + 1)
                c = chunk_size(n)
                tt(sw_hl[:, n % 2, 1, 0:c], sw_raw[:, n % 2, 0:c], sw_hl[:, n % 2, 0, 0:c].bitcast(F32), SUB)\
                    .then_inc(sw_lo, 1)

            def sum_up(b, which, m, slots, dst):
                v.wait_ge(sq_done, sq_at(b, which) + m + 1)
                if m > 1:
                    v.wait_ge(sum_done, sum_at(b, which) + m - 1)
                tt(dst, slots[0] if m == 1 else dst, slots[m % 2], ADD).then_inc(sum_done, 1)

            def reciprocal_mean(b, which, width, dst):
                for p, (t0, n) in enumerate(PIECES):
                    bank = wait_aux(v, b, (which, 0, p))
                    v.tensor_scalar(dst[:, t0:t0 + n], aux[:, bank, 0:n], 1.0 / width, EPS, MUL, ADD)\
                     .then_inc(aux_free[bank], 1)
                v.wait_ge(aux_free[bank], aux_n(b, (which, 0, LASTP)) // AUX + 1)
                v.reciprocal(dst, dst).then_inc(rec_done, 1)

            def gain_lo(b, which, k, gain, src):
                v.wait_ge(xg_hi, xg_at(b, which) + k + 1)
                stt(act_hl[:, 1, k, :], src, v1(gain + k), act_hl[:, 0, k, :].bitcast(F32), MUL, SUB).then_inc(xg_lo, 1)

            def stream_x(b, k):
                if k == 2:
                    small_lo(b * NSMALL)
                gain_lo(b, "n1", k, G_MIX, tmp[:, k % 2, :])
                if k:
                    sum_up(b, "n1", k, [tmp[:, 3, :], tmp[:, 4, :]], tmp[:, 5, :])

            def norm(b, which, gain, rstd, src, dst, lo_src, out):
                n = NCH[which]
                v.wait_ge(rstd_done, norm_n(b, which) + 1)
                for k in range(n + 1):
                    if k < n:
                        if k >= 2:
                            v.wait_ge(nrm_lo, nrm_at(b, which) + k - 1)
                        stt(dst(k), src(k), v1(gain + k), rstd, MUL, MUL).then_inc(nrm, 1)
                    if k:
                        v.wait_ge(nrm_hi, nrm_at(b, which) + k)
                        hi, lo = out(k - 1)
                        tt(lo, lo_src(k - 1), hi, SUB).then_inc(nrm_lo, 1)

            def natural(ap):
                return ap.rearrange("p s c -> p c s")

            def tokens(ap):
                return ap.rearrange("p (c s) -> p c s", s=L)

            def flat(ap):
                return ap.rearrange("p s c -> p (s c)")

            def lru_inputs(b, j):
                if b or j:
                    v.wait_ge(conv_done, b * KL + j)
                for p, (t0, n) in enumerate(PIECES):
                    bank = wait_acc(v, b, ("xl", j, p))
                    tt(xl[:, 3 + t0:3 + t0 + n], acc[:, bank, 0:n], rstd1[:, t0:t0 + n], MUL).then_inc(acc_free[bank], 1)
                wait_evacuated(v, b, ("xl", j, LASTP))
                v.tensor_copy(xl[:, 0:3], conv_st[:, j, 0, :])
                link(v.tensor_copy(xl[:, S0:S0 + 3], conv_st[:, j, 1, :]))
                v.tensor_copy(conv_st[:, j, 0, :], xl[:, TP:TP + 3])
                v.tensor_copy(conv_st[:, j, 1, :], xl[:, TB:TB + 3])

            def conv(b, j):
                if j >= 2:
                    v.wait_ge(ylru_done, b * KL + j - 1)
                xc = tmp[:, 6 + j % 2, :]
                link(v.tensor_scalar(xc, xl[:, 0:TB], v1(CONV + j), v1(CONVB + j), MUL, ADD))
                for k in range(1, CONV_W):
                    ins = stt(xc, xl[:, k:k + TB], v1(CONV + KL * k + j), xc, MUL, ADD)
                    if k < CONV_W - 1:
                        link(ins)
                ins.then_inc(conv_done, 1)

            def lru_bx(b, j):
                wait_evacuated(v, b, ("ig", j, LASTP))
                tt(tmp[:, j % 2, :], tmp[:, j % 2, :], tmp[:, 6 + j % 2, :], MUL).then_inc(bx_done, 1)

            def lru_q(b, j):
                v.wait_ge(gates_done, b * KL + j + 1)
                stt(tmp[:, 6 + j % 2, :], tmp[:, 8 + j % 2, :], 1.0, tmp[:, 6 + j % 2, :], ADD, MUL).then_inc(q_done, 1)

            def lru_scan(b, j):
                v.wait_ge(sqrt_done, b * KL + j + 1)
                bx, h, decay = tmp[:, j % 2, :], tmp[:, 6 + j % 2, :], tmp[:, 4 + j % 2, :]
                link(tt(bx, bx, h, MUL))
                v.tensor_tensor_scan(h[:, 0:S0], decay[:, 0:S0], bx[:, 0:S0], lru_st[:, j, 0:1], MUL, ADD)
                link(v.tensor_tensor_scan(h[:, S0:TB], decay[:, S0:TB], bx[:, S0:TB], lru_st[:, j, 1:2], MUL, ADD))
                v.tensor_copy(lru_st[:, j, 0:1], h[:, TP - 1:TP])
                v.tensor_copy(lru_st[:, j, 1:2], h[:, TB - 1:TB])
                v.wait_ge(glz_done, NPC * (b * KL + j + 1))
                tt(y_lru[:, j, :], y_lru[:, j, :], h, MUL).then_inc(ylru_done, 1)

            def s5_states(b, t):
                s = s5tmp[:, t % 2]
                cos = s5ring[:, t % 4, :, 5 * P:5 * P + NW]
                sin = s5ring[:, t % 4, :, 5 * P + NW:SP5]
                v.wait_ge(ring_in[t % 4], 16 * (b * 4 + t // 4 + 1))
                for n, (key, tab) in enumerate((("v1", cos), ("v2", sin))):
                    bank = wait_acc(v, b, (key, t, 0))
                    tt(s[:, n, :, 0:NC], acc[:, bank, 0:2 * NC].rearrange("p (q c) -> p q c", q=2), tab[:, :, 1:NW],
                       MUL).then_inc(acc_free[bank], 1)
                if t >= 2:
                    v.wait_ge(p_done, b * GP + t - 1)
                wait_evacuated(v, b, ("v2", t, 0))
                link(tt(s[:, 2, :, 1:NW], s[:, 0, :, 0:NC], s[:, 1, :, 0:NC], ADD))
                link(v.tensor_copy(s[:, 2, :, 0:NW:CS], carry5[:, 2 * t:2 * t + 2, :]))
                v.wait_ge(data0_done, 2 * (b * GP + t + 1))
                v.tensor_tensor_scan(s[:, 3].rearrange("p q c -> p (q c)"), s[:, 6].rearrange("p q c -> p (q c)"),
                                     s[:, 2].rearrange("p q c -> p (q c)"), 0.0, MUL, ADD).then_inc(w_done, 1)

            def gu_lo_split(b, i, q):
                v.wait_ge(gu_hi, chunk(b, i, q) + 1)
                tt(gu_hl[q][:, 1, :], f_raw[:, q, 0:2 * D], gu_hl[q][:, 0, :].bitcast(F32), SUB).then_inc(gu_lo, 1)

            def ffn(b, i, last):
                for q in range(2):
                    v.wait_ge(dn_hi, chunk(b, i, q) + 1)
                    tt(dn_hl[q][:, 1, :], f_raw[:, q, 2 * D:3 * D], dn_hl[q][:, 0, :].bitcast(F32), SUB).then_inc(dn_lo, 1)
                for q in range(2):
                    def hidden_lo(p):
                        t0, n = PIECES[p]
                        v.wait_ge(ff_hi, i * (2 * NPC) + (b * NI * 2 * NPC + q * NPC + p + 1))
                        tt(ff_hl[:, q, 1, t0:t0 + n], f_tmp[:, 3 + p, 0:n], ff_hl[:, q, 0, t0:t0 + n].bitcast(F32), SUB)\
                            .then_inc(ff_lo, 1)

                    for p, (t0, n) in enumerate(PIECES):
                        m = q * 2 * NPC + 2 * p
                        v.wait_ge(acc_full, ffn_acc(b, i, m + 1))
                        if q:
                            v.wait_ge(ff_lo, i * (2 * NPC) + (b * NI * 2 * NPC + p + 1))
                        tt(f_tmp[:, p, 0:n], acc[:, m % ACC, 0:n], rstd2[:, t0:t0 + n], MUL).then_inc(acc_free[m % ACC], 1)
                        v.wait_ge(acc_full, ffn_acc(b, i, m + 2))
                        tt(f_tmp[:, 3 + p, 0:n], acc[:, (m + 1) % ACC, 0:n], rstd2[:, t0:t0 + n], MUL)\
                            .then_inc(acc_free[(m + 1) % ACC], 1)
                        if p:
                            hidden_lo(p - 1)
                    hidden_lo(NPC - 1)
                    if not last and q == 0:
                        gu_lo_split(b, i + 1, 0)
                for p, (t0, n) in enumerate(PIECES):
                    for d in range(KD):
                        m = p * KD + d
                        bank = (b * AUX_BLOCK + AUX_FFN + m) % AUX
                        v.wait_ge(aux_full, ffn_aux(b, i, m + 1))
                        tt(x_acc[:, d, t0:t0 + n], x_acc[:, d, t0:t0 + n], aux[:, bank, 0:n], ADD).then_inc(aux_free[bank], 1)
                        if last and b + 1 < BLOCKS and m % 3 == 2:
                            stream_x(b + 1, m // 3)
                    if not last and p == 0:
                        gu_lo_split(b, i + 1, 1)

            def final_rows(b, ks):
                v.wait_ge(rstd_done, norm_n(b, "nf") + 1)
                for k in ks:
                    stt(x_acc[:, k, :], x_acc[:, k, :], v1(G_FIN + k), tmp[:, 7, :], MUL, MUL).then_inc(y_done, 1)

            for b in range(BLOCKS):
                w0 = b * NSMALL
                if b == 0:
                    for k in range(KD):
                        stream_x(b, k)
                    small_lo(w0 + 1)
                else:
                    small_lo(w0 + 1)
                    for m in range(1, KD):
                        sum_up(b - 1, "nf", m, [tmp[:, 8, :], tmp[:, 9, :]], tmp[:, 6, :])
                reciprocal_mean(b, "n1", D, rstd1[:])
                v.wait_ge(rstd_done, norm_n(b, "n1") + 1)
                for w, (kind, j) in enumerate(IN_ORDER):
                    if (kind, j) == ("xl", 2):
                        lru_bx(b, 0)
                        lru_bx(b, 1)
                    if kind == "xl":
                        lru_inputs(b, j)
                    else:
                        for p, (t0, n) in enumerate(PIECES):
                            bank = wait_acc(v, b, (kind, j, p))
                            if kind == "us":
                                tt(zs[:, j, :, t0 // L:(t0 + n) // L], acc[:, bank, 0:n].rearrange("p (c s) -> p s c", s=L),
                                   rstd1[:, t0:t0 + n].rearrange("p (c s) -> p s c", s=L), MUL).then_inc(acc_free[bank], 1)
                            else:
                                tt(y_lru[:, j, t0:t0 + n], acc[:, bank, 0:n], rstd1[:, t0:t0 + n], MUL)\
                                    .then_inc(acc_free[bank], 1)
                    if kind == "xl" and j < 2:
                        conv(b, j)
                    small_lo(w0 + w + 2)
                    if (kind, j) == ("xl", 2):
                        for i in range(2):
                            lru_q(b, i)
                        for i in range(2):
                            lru_scan(b, i)
                        conv(b, 2)
                    if (kind, j) == ("xl", 3):
                        conv(b, 3)
                    if b and kind == "us":
                        if j == 0:
                            reciprocal_mean(b - 1, "nf", D, tmp[:, 7, :])
                        elif j < 3:
                            final_rows(b - 1, range(4 * j - 4, 4 * j))
                for j in (2, 3):
                    lru_bx(b, j)
                for j in (2, 3):
                    lru_q(b, j)
                for j in (2, 3):
                    lru_scan(b, j)
                for t in range(GP):
                    s5_states(b, t)
                bank = wait_aux(v, b, ("fin", 0, 0))
                v.tensor_copy(carry5[:].rearrange("p g s -> p (g s)"), aux[:, bank, 0:2 * G]).then_inc(aux_free[bank], 1)
                for m in range(1, KL):
                    sum_up(b, "nl", m, [tmp[:, 9, :], sig2[:]], tmp[:, 8, :])
                for j in range(KL):
                    v.wait_ge(g_hi, b * KL + j + 1)
                    tt(tokens(g_hl[:, 1, j, :]), natural(zs[:, j]), tokens(g_hl[:, 0, j, :].bitcast(F32)), SUB)\
                        .then_inc(g_lo, 1)
                reciprocal_mean(b, "nl", LRU_W, tmp[:, 8, :])
                norm(b, "nl", G_LRU, tmp[:, 8, :], lambda k: y_lru[:, k, :], lambda k: y_lru[:, k, :],
                     lambda k: y_lru[:, k, :], lambda k: (act_hl[:, 0, k, :].bitcast(F32), act_hl[:, 1, k, :]))
                for j in range(KL):
                    wait_evacuated(v, b, ("glu", j, LASTP))
                    sig = btmp[:, 3, :] if j % 2 == 0 else sig2[:]
                    tt(flat(zs[:, j]), flat(zs[:, j]), sig, MUL).then_inc(yssm_done, 1)
                    small_lo(w0 + 12 + j + 2)
                    if j:
                        sum_up(b, "ns", j, [btmp[:, 0, :], btmp[:, 1, :]], btmp[:, 2, :])
                reciprocal_mean(b, "ns", SSM_W, tmp[:, 9, :])
                norm(b, "ns", G_SSM, tmp[:, 9, :], lambda k: flat(zs[:, k]), lambda k: flat(zs[:, k]),
                     lambda k: natural(zs[:, k]),
                     lambda k: (tokens(act_hl[:, 0, KL + k, :].bitcast(F32)), tokens(act_hl[:, 1, KL + k, :])))
                v.wait_ge(x_in, 16 * (b + 1))
                for d in range(KD):
                    for p, (t0, n) in enumerate(PIECES):
                        bank = wait_acc(v, b, ("out", d, p))
                        tt(x_acc[:, d, t0:t0 + n], x_acc[:, d, t0:t0 + n], acc[:, bank, 0:n], ADD).then_inc(acc_free[bank], 1)
                    if d >= 2:
                        sum_up(b, "n2", d - 1, [tmp[:, 8, :], tmp[:, 9, :]], tmp[:, 6, :])
                    if d + 2 < KD:
                        small_lo(w0 + 12 + KL + d + 2)
                    if d == 3:
                        gu_lo_split(b, 0, 0)
                for k in range(KD):
                    gain_lo(b, "n2", k, G_FFN, x_acc[:, k, :])
                    if k == 1:
                        sum_up(b, "n2", KD - 1, [tmp[:, 8, :], tmp[:, 9, :]], tmp[:, 6, :])
                gu_lo_split(b, 0, 1)
                reciprocal_mean(b, "n2", D, rstd2[:])
                v.wait_ge(rstd_done, norm_n(b, "n2") + 1)
                with v.Fori(0, NI - 1) as i:
                    ffn(b, i, False)
                ffn(b, NI - 1, True)
            for m in range(1, KD):
                sum_up(BLOCKS - 1, "nf", m, [tmp[:, 8, :], tmp[:, 9, :]], tmp[:, 6, :])
            reciprocal_mean(BLOCKS - 1, "nf", D, tmp[:, 7, :])
            final_rows(BLOCKS - 1, range(KD))


def _layout(inp):
    import numpy as np

    f = {k: np.asarray(x)[0] if k not in ("x_prompt", "x_sample", "norm_final") else np.asarray(x)
         for k, x in inp.items()}
    out = {}
    xs = np.zeros((BLOCKS, TB, D), np.float32)
    for b in range(BLOCKS):
        xs[b, 0:TP] = f["x_prompt"][0, b * TP:(b + 1) * TP]
        xs[b, S0:TB] = f["x_sample"][0, b * TS:(b + 1) * TS]
    out["x"] = xs.reshape(BLOCKS, TB, KD, P).transpose(0, 3, 2, 1)

    def chunks(w):
        return w.reshape(w.shape[0] // P, P, w.shape[1] // P, P).transpose(2, 1, 0, 3).reshape(w.shape[1] // P, P, -1)

    at = {"xl": 0, "gl": KL, "us": 2 * KL}
    out["w_in"] = chunks(f["w_in"])[[at[k] + j for k, j in IN_ORDER]]
    out["w_glu"] = chunks(f["ssm_w_glu"])
    out["w_out"] = chunks(f["w_out"])
    out["w_ffn"] = np.concatenate([chunks(f["w_gate"]), chunks(f["w_up"]), f["w_down"].reshape(NF, P, D)], axis=2)

    def cols(x):
        return x.reshape(-1, P).T

    out["vec"] = np.concatenate([cols(f[k]) for k in ("norm_mix", "norm_ffn", "norm_final", "norm_lru_out", "norm_ssm_out",
                                                      "lru_ba", "lru_bx", "ssm_b_glu")]
                                + [cols(f["conv_w"][k]) for k in range(CONV_W)] + [cols(f["conv_b"]), cols(f["lru_lambda"])],
                                axis=1)
    wg = np.zeros((P, 2, KL, P), np.float32)
    for g, k in enumerate(("lru_wa", "lru_wx")):
        for h in range(8):
            o = 64 * (h % 2)
            wg[o:o + 64, g, h // 2, o:o + 64] = f[k][h]
    out["w_gates"] = wg

    def two(re, im):
        return np.concatenate([np.moveaxis(re, 1, 0), np.moveaxis(im, 1, 0)], axis=0)

    lr, li = f["ssm_lambda_re"], f["ssm_lambda_im"]
    out["p5"] = np.stack([two(lr, lr), two(li, li), np.broadcast_to(f["ssm_log_dt"], (P, G))], axis=1)
    br, bi = f["ssm_b_re"], f["ssm_b_im"]
    cr, ci = f["ssm_c_re"].transpose(0, 2, 1), f["ssm_c_im"].transpose(0, 2, 1)
    out["bc"] = np.stack([two(br, bi), two(bi, br), two(cr, ci), two(ci, cr)], axis=1)
    out["dsk"] = f["ssm_d"].reshape(G, HG).T
    c5 = np.zeros((P, G, 2), np.float32)
    c5[:, :, 1] = two(f["state_ssm_re"][0], f["state_ssm_im"][0])
    out["carry5"] = c5
    cs = np.zeros((P, KL, 2, CONV_W - 1), np.float32)
    cs[:, :, 1, :] = f["state_conv"][0].reshape(CONV_W - 1, KL, P).transpose(2, 1, 0)
    out["conv_st"] = cs
    ls = np.zeros((P, KL, 2), np.float32)
    ls[:, :, 1] = cols(f["state_lru"][0])
    out["lru_st"] = ls
    out["ident"] = np.eye(P, dtype=np.float32)
    out["swap"] = np.roll(np.eye(P, dtype=np.float32), NP_, axis=0)
    mask = np.ones(NW, np.float32)
    mask[[0, CS]] = 0
    out["lmask"] = np.broadcast_to(mask, (P, NW))
    out["jrow"] = np.broadcast_to(np.concatenate([np.arange(CS), np.arange(NW - CS)]).astype(np.float32), (P, NW))
    out["kf"] = np.broadcast_to(np.array([7, 6, 5, 4, 3, 2, 1, 0, *range(9)], np.float32), (P, NPOW))
    out["sgn"] = np.where(np.arange(P) < NP_, -1, 1).astype(np.float32)[:, None]
    return {k: np.ascontiguousarray(x) for k, x in out.items()}


def kernel(**inputs):
    import numpy as np
    import concourse.bacc as bacc
    from concourse.bass_utils import run_bass_kernel_spmd

    nc = bacc.Bacc("TRN2", target_bir_lowering=False, num_devices=1)
    arrays = {f"in_{k}": x for k, x in _layout(inputs).items()}
    a = {k[3:]: nc.dram_tensor(k, x.shape, F32, kind="ExternalInput").ap() for k, x in arrays.items()}
    shapes = {"y": (BLOCKS, P, KD, TB), "s5": (P, G, 2), "conv": (P, KL, 2, CONV_W - 1), "lru": (P, KL, 2)}
    outs = {k: nc.dram_tensor(f"out_{k}", s, F32, kind="ExternalOutput").ap() for k, s in shapes.items()}
    build(nc, a, outs)
    r = run_bass_kernel_spmd(nc, [arrays], core_ids=[0]).results[0]
    y, s5, conv, lru = (np.asarray(r[f"out_{k}"]) for k in ("y", "s5", "conv", "lru"))
    y = y.transpose(0, 3, 2, 1).reshape(BLOCKS, TB, D)
    y_prompt = np.ascontiguousarray(y[:, 0:TP].reshape(1, SEQ, D))
    y_sample = np.ascontiguousarray(y[:, S0:TB].reshape(1, DEC_SEQ, D))
    states = []
    for s in range(2):
        c = conv[:, :, s, :].transpose(2, 1, 0).reshape(1, 1, CONV_W - 1, LRU_W)
        h = lru[:, :, s].T.reshape(1, 1, LRU_W)
        re, im = s5[0:NP_, :, s].T[None, None], s5[NP_:P, :, s].T[None, None]
        states += [np.ascontiguousarray(x) for x in (c, h, re, im)]
    return (y_prompt, y_sample, *states)
```
